# Optimizing a Trainium2 kernel written in Bass

```python
import math
import jax, jax.numpy as jnp
from jax import lax
import numpy as np

D_MODEL = 1024
BATCH = 1
SEQ = 512
DEPTH = 2

MIX_WIDTH = D_MODEL
A_HEADS = 6
A_QK_DIM = 32
A_V_DIM = 2 * A_QK_DIM
A_WIDTH = A_HEADS * A_V_DIM
POOL_WINDOWS = (2, 4, 8, 16)
POOL_GROUP_DIM = 64
POOL_GROUPS = len(POOL_WINDOWS)
POOL_WIDTH = POOL_GROUPS * POOL_GROUP_DIM
C_HEADS = 6
C_KV_GROUPS = 2
C_HEADS_PER_GROUP = C_HEADS // C_KV_GROUPS
C_HEAD_DIM = 64
C_WIDTH = C_HEADS * C_HEAD_DIM
C_KV_WIDTH = C_KV_GROUPS * C_HEAD_DIM
CMP_BLOCK = 32
CMP_STRIDE = 16
SEL_BLOCK = 64
N_SEL = 16
WINDOW = 512
N_BRANCH = 3
FORCED_SCORE = 1.0e4
D_FF = 4 * D_MODEL
ROPE_THETA = 10000.0
LN_EPS = 1e-5
RMS_EPS = 1e-6
ALPHA = (2 * DEPTH) ** 0.25
BETA = (8 * DEPTH) ** -0.25
Q_BLOCK = 128
NSA_Q_BLOCK = 64

IN_SPLITS = (A_HEADS * 2 * A_QK_DIM,
             A_HEADS * 2 * A_QK_DIM,
             A_WIDTH,
             POOL_WIDTH,
             C_WIDTH,
             C_KV_WIDTH, C_KV_WIDTH,
             C_KV_WIDTH, C_KV_WIDTH,
             C_KV_WIDTH, C_KV_WIDTH,
             C_HEADS * N_BRANCH)
N_IN = sum(IN_SPLITS)

kernel_name = "hymba_diffattn_pool_nsa_deepnorm"

def layer_norm(x, g, b):
    xf = x.astype(jnp.float32)
    mu = jnp.mean(xf, -1, keepdims=True)
    var = jnp.mean(jnp.square(xf - mu), -1, keepdims=True)
    y = (xf - mu) * lax.rsqrt(var + LN_EPS) * g.astype(jnp.float32) + b.astype(jnp.float32)
    return y.astype(x.dtype)

def rope_tables(seq, dim):
    inv = 1.0 / (ROPE_THETA ** (jnp.arange(0, dim, 2, dtype=jnp.float32) / dim))
    ang = jnp.arange(seq, dtype=jnp.float32)[:, None] * inv[None, :]
    return jnp.cos(ang), jnp.sin(ang)

def apply_rope(x, cos, sin):
    xf = x.astype(jnp.float32)
    x1, x2 = jnp.split(xf, 2, axis=-1)
    return jnp.concatenate([x1 * cos - x2 * sin, x2 * cos + x1 * sin], -1).astype(x.dtype)

def masked_softmax(sc, mask):
    sc = sc.astype(jnp.float32)
    p = jax.nn.softmax(jnp.where(mask, sc, -1e30), axis=-1)
    return jnp.where(mask, p, 0.0)

def diff_attention(q1, q2, k1, k2, v, lam, lam_init, subln_g):
    B, H, T, dq = q1.shape
    scale = dq ** -0.5
    kpos = jnp.arange(T)

    def block(i):
        s = i * Q_BLOCK
        qpos = s + jnp.arange(Q_BLOCK)
        mask = kpos[None, :] <= qpos[:, None]

        def probs(q, k):
            qb = lax.dynamic_slice_in_dim(q, s, Q_BLOCK, axis=2)
            sc = jnp.einsum('bhqd,bhkd->bhqk', qb, k).astype(jnp.float32) * scale
            return jax.nn.softmax(jnp.where(mask, sc, -jnp.inf), axis=-1)

        p = probs(q1, k1) - lam * probs(q2, k2)
        return jnp.einsum('bhqk,bhkd->bhqd', p.astype(v.dtype), v)

    o = lax.map(block, jnp.arange(T // Q_BLOCK))
    o = jnp.transpose(o, (1, 0, 3, 2, 4)).reshape(B, T, H, -1)
    of = o.astype(jnp.float32)
    of = of * lax.rsqrt(jnp.mean(jnp.square(of), -1, keepdims=True) + RMS_EPS)
    of = of * subln_g.astype(jnp.float32) * (1.0 - lam_init)
    return of.reshape(B, T, -1).astype(v.dtype)

def pool_mixer(u, w_pool, pool_scale):
    B, T, _ = u.shape
    uf = u.astype(jnp.float32).reshape(B, T, POOL_GROUPS, POOL_GROUP_DIM)
    csum = jnp.pad(jnp.cumsum(uf, axis=1), ((0, 0), (1, 0), (0, 0), (0, 0)))
    t = jnp.arange(T)
    means = []
    for g, w in enumerate(POOL_WINDOWS):
        lo = jnp.maximum(t + 1 - w, 0)
        cnt = jnp.minimum(t + 1, w).astype(jnp.float32)
        means.append((csum[:, 1:, g] - csum[:, lo, g]) / cnt[None, :, None])
    y = jnp.stack(means, axis=2) - uf
    y = jnp.einsum('btgc,gcd->btgd', y, w_pool.astype(jnp.float32))
    y = y.reshape(B, T, POOL_WIDTH) * pool_scale.astype(jnp.float32)
    return y.astype(u.dtype)

def _gather_blocks(blocks, idx):
    return blocks[idx]

def nsa_attention(q, k_cmp, v_cmp, k_slc, v_slc, k_win, v_win, gates,
                  pe_k, pe_v, w_ck, w_cv):
    B, G, h, T, d = q.shape
    scale = d ** -0.5
    n_cmp = (T - CMP_BLOCK) // CMP_STRIDE + 1
    cmp_start = jnp.arange(n_cmp) * CMP_STRIDE
    cmp_idx = cmp_start[:, None] + jnp.arange(CMP_BLOCK)[None, :]
    kc = jnp.einsum('bgnld,lde->bgne', k_cmp[:, :, cmp_idx] + pe_k, w_ck)
    vc = jnp.einsum('bgnld,lde->bgne', v_cmp[:, :, cmp_idx] + pe_v, w_cv)
    cmp_end = cmp_start + CMP_BLOCK - 1
    n_blk = T // SEL_BLOCK
    n_sel = min(N_SEL, n_blk)
    blk_start = jnp.arange(n_blk) * SEL_BLOCK
    overlap = ((cmp_start[:, None] < blk_start[None, :] + SEL_BLOCK)
               & (cmp_start[:, None] + CMP_BLOCK > blk_start[None, :])).astype(jnp.float32)
    k_blocks = k_slc.reshape(B, G, n_blk, SEL_BLOCK, d)
    v_blocks = v_slc.reshape(B, G, n_blk, SEL_BLOCK, d)
    gather = jax.vmap(jax.vmap(_gather_blocks))
    pad = ((0, 0), (0, 0), (WINDOW, 0), (0, 0))
    k_win_p = jnp.pad(k_win, pad)
    v_win_p = jnp.pad(v_win, pad)
    blk_ids = jnp.arange(n_blk)[None, :]

    def block(i):
        s = i * NSA_Q_BLOCK
        t = s + jnp.arange(NSA_Q_BLOCK)
        qb = lax.dynamic_slice_in_dim(q, s, NSA_Q_BLOCK, axis=3)
        cmask = cmp_end[None, :] <= t[:, None]
        p_cmp = masked_softmax(jnp.einsum('bghqd,bgnd->bghqn', qb, kc) * scale, cmask)
        o_cmp = jnp.einsum('bghqn,bgnd->bghqd', p_cmp.astype(vc.dtype), vc)
        imp = jnp.einsum('bghqn,ns->bgqs', p_cmp, overlap)
        cur = (t // SEL_BLOCK)[:, None]
        forced = (blk_ids == 0) | (blk_ids == cur) | (blk_ids == cur - 1)
        imp = jnp.where(forced, FORCED_SCORE, imp)
        imp = jnp.where(blk_ids > cur, -1.0, imp)
        _, sel = lax.top_k(imp, n_sel)
        ks = gather(k_blocks, sel).reshape(B, G, NSA_Q_BLOCK, n_sel * SEL_BLOCK, d)
        vs = gather(v_blocks, sel).reshape(B, G, NSA_Q_BLOCK, n_sel * SEL_BLOCK, d)
        kpos = (sel[..., None] * SEL_BLOCK + jnp.arange(SEL_BLOCK)).reshape(
            B, G, NSA_Q_BLOCK, n_sel * SEL_BLOCK)
        smask = (kpos <= t[None, None, :, None])[:, :, None]
        p_slc = masked_softmax(jnp.einsum('bghqd,bgqkd->bghqk', qb, ks) * scale, smask)
        o_slc = jnp.einsum('bghqk,bgqkd->bghqd', p_slc.astype(vs.dtype), vs)
        kw = lax.dynamic_slice_in_dim(k_win_p, s, WINDOW + NSA_Q_BLOCK, axis=2)
        vw = lax.dynamic_slice_in_dim(v_win_p, s, WINDOW + NSA_Q_BLOCK, axis=2)
        wpos = s - WINDOW + jnp.arange(WINDOW + NSA_Q_BLOCK)
        wmask = ((wpos[None, :] <= t[:, None]) & (wpos[None, :] > t[:, None] - WINDOW)
                 & (wpos[None, :] >= 0))
        p_win = masked_softmax(jnp.einsum('bghqd,bgkd->bghqk', qb, kw) * scale, wmask)
        o_win = jnp.einsum('bghqk,bgkd->bghqd', p_win.astype(vw.dtype), vw)
        return jnp.stack([o_cmp, o_slc, o_win], axis=-1)

    o = lax.map(block, jnp.arange(T // NSA_Q_BLOCK))
    o = jnp.transpose(o, (1, 0, 4, 2, 3, 5, 6)).reshape(B, T, G, h, d, N_BRANCH)
    out = jnp.einsum('btghdr,btghr->btghd', o, gates)
    return out.reshape(B, T, G * h * d)

def _to_kv(z, B, T):
    return z.reshape(B, T, C_KV_GROUPS, C_HEAD_DIM).transpose(0, 2, 1, 3)

def setup_inputs(seed: int = 0) -> dict:
    key = jax.random.key(seed)
    ks = jax.random.split(key, 22)

    def nrm(k, shape, s):
        return jax.random.normal(k, shape, jnp.float32) * s

    return {
        'x': nrm(ks[0], (BATCH, SEQ, D_MODEL), 1.0),
        'w_in': nrm(ks[1], (DEPTH, D_MODEL, N_IN), D_MODEL ** -0.5),
        'lam_q1': nrm(ks[2], (DEPTH, A_QK_DIM), 0.1),
        'lam_k1': nrm(ks[3], (DEPTH, A_QK_DIM), 0.1),
        'lam_q2': nrm(ks[4], (DEPTH, A_QK_DIM), 0.1),
        'lam_k2': nrm(ks[5], (DEPTH, A_QK_DIM), 0.1),
        'subln_g': 1.0 + nrm(ks[6], (DEPTH, A_V_DIM), 0.02),
        'w_pool': nrm(ks[7], (DEPTH, POOL_GROUPS, POOL_GROUP_DIM, POOL_GROUP_DIM), POOL_GROUP_DIM ** -0.5),
        'pool_scale': 1.0 + nrm(ks[8], (DEPTH, POOL_WIDTH), 0.1),
        'cmp_pe_k': nrm(ks[9], (DEPTH, CMP_BLOCK, C_HEAD_DIM), 0.1),
        'cmp_pe_v': nrm(ks[10], (DEPTH, CMP_BLOCK, C_HEAD_DIM), 0.1),
        'w_cmp_k': nrm(ks[11], (DEPTH, CMP_BLOCK, C_HEAD_DIM, C_HEAD_DIM), (CMP_BLOCK * C_HEAD_DIM) ** -0.5),
        'w_cmp_v': nrm(ks[12], (DEPTH, CMP_BLOCK, C_HEAD_DIM, C_HEAD_DIM), (CMP_BLOCK * C_HEAD_DIM) ** -0.5),
        'w_out': nrm(ks[13], (DEPTH, MIX_WIDTH, D_MODEL), BETA * MIX_WIDTH ** -0.5),
        'ln1_g': 1.0 + nrm(ks[14], (DEPTH, D_MODEL), 0.02),
        'ln1_b': nrm(ks[15], (DEPTH, D_MODEL), 0.02),
        'w_up': nrm(ks[16], (DEPTH, D_MODEL, D_FF), D_MODEL ** -0.5),
        'w_down': nrm(ks[17], (DEPTH, D_FF, D_MODEL), BETA * D_FF ** -0.5),
        'ln2_g': 1.0 + nrm(ks[18], (DEPTH, D_MODEL), 0.02),
        'ln2_b': nrm(ks[19], (DEPTH, D_MODEL), 0.02),
    }

def reference(x, w_in, lam_q1, lam_k1, lam_q2, lam_k2, subln_g, w_pool, pool_scale,
              cmp_pe_k, cmp_pe_v, w_cmp_k, w_cmp_v, w_out, ln1_g, ln1_b,
              w_up, w_down, ln2_g, ln2_b):
    B, T, _ = x.shape
    G, h = C_KV_GROUPS, C_HEADS_PER_GROUP
    cos_a, sin_a = rope_tables(T, A_QK_DIM)
    cos_c, sin_c = rope_tables(T, C_HEAD_DIM)
    offsets = np.cumsum(IN_SPLITS)[:-1].tolist()
    for l in range(DEPTH):
        lam_init = 0.8 - 0.6 * math.exp(-0.3 * l)
        proj = jnp.einsum('btd,dn->btn', x, w_in[l])
        (qa, ka, va, u, qc, kcm, vcm, ksl, vsl, kwi, vwi, gc) = jnp.split(proj, offsets, axis=-1)
        qa = apply_rope(qa.reshape(B, T, A_HEADS, 2, A_QK_DIM).transpose(0, 2, 3, 1, 4), cos_a, sin_a)
        ka = apply_rope(ka.reshape(B, T, A_HEADS, 2, A_QK_DIM).transpose(0, 2, 3, 1, 4), cos_a, sin_a)
        va = va.reshape(B, T, A_HEADS, A_V_DIM).transpose(0, 2, 1, 3)
        lam = (jnp.exp(jnp.sum(lam_q1[l].astype(jnp.float32) * lam_k1[l].astype(jnp.float32)))
               - jnp.exp(jnp.sum(lam_q2[l].astype(jnp.float32) * lam_k2[l].astype(jnp.float32)))
               + lam_init)
        o_a = diff_attention(qa[:, :, 0], qa[:, :, 1], ka[:, :, 0], ka[:, :, 1], va,
                             lam, lam_init, subln_g[l])
        o_b = pool_mixer(u, w_pool[l], pool_scale[l])
        qc = apply_rope(qc.reshape(B, T, G, h, C_HEAD_DIM).transpose(0, 2, 3, 1, 4), cos_c, sin_c)
        kcm = apply_rope(_to_kv(kcm, B, T), cos_c, sin_c)
        ksl = apply_rope(_to_kv(ksl, B, T), cos_c, sin_c)
        kwi = apply_rope(_to_kv(kwi, B, T), cos_c, sin_c)
        gates = jax.nn.sigmoid(gc.astype(jnp.float32)).astype(x.dtype).reshape(B, T, G, h, N_BRANCH)
        o_c = nsa_attention(qc, kcm, _to_kv(vcm, B, T), ksl, _to_kv(vsl, B, T),
                            kwi, _to_kv(vwi, B, T), gates,
                            cmp_pe_k[l], cmp_pe_v[l], w_cmp_k[l], w_cmp_v[l])
        mix = jnp.einsum('btm,md->btd', jnp.concatenate([o_a, o_b, o_c], axis=-1), w_out[l])
        x = layer_norm(ALPHA * x + mix, ln1_g[l], ln1_b[l])
        hid = jnp.square(jax.nn.relu(jnp.einsum('btd,df->btf', x, w_up[l])))
        x = layer_norm(ALPHA * x + jnp.einsum('btf,fd->btd', hid, w_down[l]), ln2_g[l], ln2_b[l])
    return x


_drawn_inputs = setup_inputs


def setup_inputs(seed=0):
    import zlib

    import numpy as np

    out = dict(_drawn_inputs(seed))
    spreads = {}
    factors = {'lam_q1': 2.785,
     'lam_k1': 3.65,
     'lam_q2': 4.552,
     'subln_g': 8.0,
     'pool_scale': 2.735,
     'cmp_pe_k': 8.0,
     'cmp_pe_v': 3.469}
    for name, (base, spread) in spreads.items():
        noise = np.random.default_rng([zlib.crc32(name.encode()), seed]).standard_normal(out[name].shape)
        drawn = base * np.exp(spread * noise) if base else spread * noise
        out[name] = __import__('jax').numpy.asarray(drawn.astype(out[name].dtype))
    for name, factor in factors.items():
        out[name] = (out[name] * factor).astype(out[name].dtype)
    return out
```

```python
from contextlib import ExitStack

import numpy as np

from concourse import mybir

F32 = mybir.dt.float32
F32R = mybir.dt.float32r
BF16 = mybir.dt.bfloat16
ALU = mybir.AluOpType
ACT = mybir.ActivationFunctionType
AX = mybir.AxisListType

P = 128
SEQ, D, DEPTH, DFF = 512, 1024, 2, 4096
TT = SEQ // P
KT = D // P
A_HEADS, A_DQ, DV = 6, 32, 64
C_HEADS, HG = 6, 3
N_IN = 2578
GATES = 18
WINDOWS = (2, 4, 8, 16)
N_CMP, CMP_L = 31, 32
ALPHA = (2 * DEPTH) ** 0.25
LN_EPS, RMS_EPS = 1e-5, 1e-6
A_SCALE, C_SCALE = A_DQ ** -0.5, 64 ** -0.5
NEG = -1.0e30

O_VA, O_U, O_QC, O_KCM, O_VCM, O_KSL, O_VSL, O_KWI, O_VWI, O_G = (
    768, 1152, 1408, 1792, 1920, 2048, 2176, 2304, 2432, 2560)
T_QA, T_KA, T_VCM, T_U, T_QC, T_KCM, T_KSL, T_KWI, T_END = 0, 384, 768, 896, 1152, 1536, 1664, 1792, 1920
V_A, V_SL, V_WI, V_END = 0, 384, 512, 640
PIECES = ((0, 768, True, T_QA), (O_VA, 384, False, V_A), (O_U, 256, True, T_U),
          *((O_QC + 64 * h, 64, True, T_QC + 128 * (h % HG) + 64 * (h // HG)) for h in range(C_HEADS)),
          (O_KCM, 128, True, T_KCM), (O_VCM, 128, True, T_VCM), (O_KSL, 128, True, T_KSL),
          (O_VSL, 128, False, V_SL), (O_KWI, 128, True, T_KWI), (O_VWI, 128, False, V_WI))
Q_VCM, Q_U, Q_QC, Q_KCM, Q_KSL, Q_KWI, Q_N = 6, 7, 9, 12, 13, 14, 15

IN_ORDER = (0, 1, 4, 3, 2)
N_MLP = 16
MLP = (("up", 0), ("up", 1), ("up", 2), ("up", 3), ("down", 0), ("down", 1), ("up", 4), ("up", 5),
       ("down", 2), ("down", 3), ("up", 6), ("up", 7), ("down", 4), ("down", 5), ("down", 6), ("down", 7))
U_IN, U_OUT, U_MLP = 0, 20, 28
UNITS = U_MLP + 4 * N_MLP
RING = 4
TASKS_A = A_HEADS * TT
TASKS = TASKS_A + C_HEADS * TT

K_ID, K_BLK = 0, 128
K_ROPE = 256
ROPE_W = 16 + 32 + 16 + 32 + 32 + 64 + 32 + 64
R_CAQ, R_SAQ, R_CAK, R_SAK, R_CCK, R_SCK, R_CCQ, R_SCQ = 0, 16, 48, 64, 96, 128, 192, 224
K_INV = K_ROPE + TT * ROPE_W
K_CM = K_INV + 2 * SEQ
K_CB = K_CM + TT * 32
K_LAM = K_CB + TT * 32
K_HALF = K_LAM + 2 * DEPTH
K_END = K_HALF + 1
K_MASK = K_END


def shape_constants():
    k = np.zeros((P, K_MASK + P), np.float32)
    p = np.arange(P)
    k[:, K_ID:K_ID + P] = np.eye(P)
    k[:, K_BLK:K_BLK + P] = (p[:, None] // 64 == p[None, :] // 64)
    k[:, K_MASK:K_MASK + P] = np.where(p[None, :] > p[:, None], NEG, 0.0)
    t = (np.arange(TT)[None, :] * P + p[:, None])

    def table(dim):
        inv = np.float32(1.0) / np.float32(10000.0) ** (np.arange(0, dim, 2, dtype=np.float32) / np.float32(dim))
        ang = np.arange(SEQ, dtype=np.float32)[:, None] * inv[None, :].astype(np.float32)
        c, s = np.cos(ang)[t], np.sin(ang)[t]
        return c, np.concatenate([-s, s], -1)

    (ca, sa), (cc, sc) = table(A_DQ), table(64)
    rope = np.concatenate([ca * A_SCALE, sa * A_SCALE, ca, sa, cc, sc, cc * C_SCALE, sc * C_SCALE], -1)
    k[:, K_ROPE:K_INV] = rope.reshape(P, -1)
    tt = np.arange(SEQ)
    for c in range(2):
        for half in range(2):
            cnt = np.minimum(tt + 1, WINDOWS[2 * c + half])
            k[64 * half:64 * half + 64, K_INV + c * SEQ:K_INV + (c + 1) * SEQ] = 1.0 / cnt
    n = np.arange(32)
    seen = (n[None, None, :] < N_CMP) & (16 * n[None, None, :] + 31 <= t[:, :, None])
    k[:, K_CM:K_CB] = seen.reshape(P, -1)
    k[:, K_CB:K_LAM] = np.where(seen, 0.0, NEG).reshape(P, -1)
    for l in range(DEPTH):
        lam_init = 0.8 - 0.6 * np.exp(-0.3 * l)
        k[:, K_LAM + 2 * l] = lam_init
        k[:, K_LAM + 2 * l + 1] = 1.0 - lam_init
    k[:, K_HALF] = -0.5
    return k


PER_LAYER = dict(
    raw=16 * UNITS // RING,
    hi_ready=UNITS, lo_ready=UNITS, unit_used=UNITS,
    x_normed=2 * TT, out_normed=TT, xt_turned=2 * KT, xt_scaled=2 * KT, xt_ready=2 * KT,
    params=16 * 22, par_turned=1, par_ready=1, gw_hi=1, gw_lo=1, lam_dot=1, lam_exp=1,
    in_copied=5 * TT, roped_a=TT, roped_c=TT, gates_turned=1, exp_gates=1,
    turned=Q_N, turned_act=8, turned_dve=7,
    cmp_rows=1, cmp_kv=1, cmp_kv_copied=1, cmp_scores=1, cmp_biased=1, cmp_shifted=1, cmp_exp=1, cmp_probs=1,
    cmp_turned=1, cmp_copied=1,
    pool_y=2, pool_mm=2, pool_scaled=2, pool_hi=2, pool_mixed=2,
    scores=TASKS, negmax=TASKS, exped=TASKS, probs=TASKS, p_turned=TASKS, p_copied_act=TASKS,
    p_copied_dve=TASKS - TASKS_A, pv=TASKS,
    oa_copied=3, oa_squared=3, ss_ready=3, ss_copied=3, rms_ready=1, oa_normed=3, oa_hi=3, oa_mixed=3,
    oc_hi=3, oc_mixed=3,
    stats=2 * TT, rstd=2 * TT, rows=64, rows_used=1, hid_hi=32, hid_ready=32, mlp_evac=4 * N_MLP,
)

CHUNKS = [("in", c) for c in IN_ORDER] + [("out", 0), ("out", 1)] + list(MLP)


def build(nc, x, w_in, lam_q1, lam_k1, lam_q2, lam_k2, subln_g, w_pool, pool_scale, cmp_pe_k, cmp_pe_v,
          w_cmp_k, w_cmp_v, w_out, ln1_g, ln1_b, w_up, w_down, ln2_g, ln2_b, consts, out):
    ctx = ExitStack()
    with ctx:
        top = [16512]

        def at(name, offset, shape, dt=F32):
            return nc.alloc_sbuf_tensor_at(name, [P] + list(shape), dt, offset=offset)

        def room(nbytes):
            top[0] += nbytes
            return top[0] - nbytes

        def sb(name, shape, dt=F32):
            size = int(np.prod(shape)) * (2 if dt == BF16 else 4)
            return at(name, room((size + 31) // 32 * 32), shape, dt)

        kc = sb("kc", [K_END])
        ident = kc[:, K_ID:K_ID + P]
        blk_ones = kc[:, K_BLK:K_BLK + P]
        ident16 = sb("ident16", [P], BF16)
        mask16 = sb("mask16", [P], BF16)
        xres = sb("xres", [TT, D])
        raw = sb("raw", [RING, 1024])
        w_hi = sb("w_hi", [RING, 1024], F32R)
        w_lo = sb("w_lo", [RING, 1024], F32R)
        ra = room(32768)
        xt_hi, xt_lo = at("xt_hi", ra, [KT, SEQ], F32R), at("xt_lo", ra + 16384, [KT, SEQ], F32R)
        qkt, upad = at("qkt", ra, [Q_N - 2, SEQ]), at("upad", ra + 2048 * (Q_N - 2), [2, 16 + SEQ])
        mt_hi, mt_lo = sb("mt_hi", [KT, SEQ], F32R), sb("mt_lo", [KT, SEQ], F32R)
        rc = room(32768)
        he_hi, he_lo = at("he_hi", rc, [KT, SEQ], F32R), at("he_lo", rc + 16384, [KT, SEQ], F32R)
        proj_t = at("proj_t", rc, [TT, T_END])
        probs = at("probs", rc, [2, 2, SEQ])
        p_t = at("p_t", rc + 8192, [2, 2, 4 * P])
        cmp_in = at("cmp_in", rc + 16384, [2, 16 * 64])
        cmp_s = at("cmp_s", rc + 16384, [TT * 6, 32])
        cmp_pt = at("cmp_pt", rc + 19456, [TT, 2, P])
        boxb = at("boxb", rc + 24576, [2, 16 + SEQ])
        boxc = at("boxc", rc + 28800, [16 + SEQ])
        proj_v = sb("proj_v", [TT, V_END])
        rd = room(12288)
        oa, rms = at("oa", rd, [3, SEQ]), at("rms", rd + 6144, [3, SEQ])
        rows, tmp = at("rows", rd, [2, D]), at("tmp", rd + 8192, [2, 512])
        w_cmp = sb("w_cmp", [2, 16 * 64])
        w_blk = sb("w_blk", [2, P])
        gw_raw, gw_hi, gw_lo = sb("gw_raw", [KT, GATES]), sb("gw_hi", [KT, GATES], F32R), sb("gw_lo", [KT, GATES], F32R)
        ln_raw = sb("ln_raw", [P])
        pe_raw = sb("pe_raw", [2, 2 * 64])
        lnp = sb("lnp", [4, KT])
        pe_t = sb("pe_t", [2, 32])
        lamv = sb("lamv", [4, 32])
        lams = sb("lams", [8])
        subg = sb("subg", [2])
        psc = sb("psc", [2])
        gates = sb("gates", [TT, GATES])
        kcmp, vcmp = sb("kcmp", [64]), sb("vcmp", [64])
        bst, mv = sb("bst", [TT, 2, 6]), sb("mv", [TT, 2])
        rstd = sb("rstd", [TT])
        negmax, sums, recs, facs = (sb(n, [4, 2]) for n in ("negmax", "sums", "recs", "facs"))
        cst = sb("cst", [4, TT * 6])
        assert top[0] <= 229368, top[0]
        ps = ctx.enter_context(nc.psum_tensor("ps", [P, 8, 512], F32))

        def sem(name):
            return ctx.enter_context(nc.semaphore(name))

        def nth(name, layer, n):
            return layer * PER_LAYER[name] + n

        s_raw = [sem(f"raw{r}") for r in range(RING)]
        s_const_in = sem("const_in")
        s_x_in = sem("x_in")
        s_masks = sem("masks")
        s_blk_zero = sem("blk_zero")
        s_chain_dve = sem("chain_dve")
        s_chain_act = sem("chain_act")
        s_chain_pool = sem("chain_pool")
        s_stored = sem("stored")
        s_hi_ready = sem("hi_ready")
        s_lo_ready = sem("lo_ready")
        s_unit_used = sem("unit_used")
        s_x_normed = sem("x_normed")
        s_out_normed = sem("out_normed")
        s_xt_turned = sem("xt_turned")
        s_xt_scaled = sem("xt_scaled")
        s_xt_ready = sem("xt_ready")
        s_params = sem("params")
        s_par_turned = sem("par_turned")
        s_par_ready = sem("par_ready")
        s_gw_hi = sem("gw_hi")
        s_gw_lo = sem("gw_lo")
        s_lam_dot = sem("lam_dot")
        s_lam_exp = sem("lam_exp")
        s_in_copied = sem("in_copied")
        s_roped_a = sem("roped_a")
        s_roped_c = sem("roped_c")
        s_gates_turned = sem("gates_turned")
        s_exp_gates = sem("exp_gates")
        s_turned = sem("turned")
        s_turned_act = sem("turned_act")
        s_turned_dve = sem("turned_dve")
        s_cmp_rows = sem("cmp_rows")
        s_cmp_kv = sem("cmp_kv")
        s_cmp_kv_copied = sem("cmp_kv_copied")
        s_cmp_scores = sem("cmp_scores")
        s_cmp_biased = sem("cmp_biased")
        s_cmp_shifted = sem("cmp_shifted")
        s_cmp_exp = sem("cmp_exp")
        s_cmp_probs = sem("cmp_probs")
        s_cmp_turned = sem("cmp_turned")
        s_cmp_copied = sem("cmp_copied")
        s_pool_y = sem("pool_y")
        s_pool_mm = sem("pool_mm")
        s_pool_scaled = sem("pool_scaled")
        s_pool_hi = sem("pool_hi")
        s_pool_mixed = sem("pool_mixed")
        s_scores = sem("scores")
        s_negmax = sem("negmax")
        s_exped = sem("exped")
        s_probs = sem("probs")
        s_p_turned = sem("p_turned")
        s_p_copied_act = sem("p_copied_act")
        s_p_copied_dve = sem("p_copied_dve")
        s_pv = sem("pv")
        s_oa_copied = sem("oa_copied")
        s_oa_squared = sem("oa_squared")
        s_ss_ready = sem("ss_ready")
        s_ss_copied = sem("ss_copied")
        s_rms_ready = sem("rms_ready")
        s_oa_normed = sem("oa_normed")
        s_oa_hi = sem("oa_hi")
        s_oa_mixed = sem("oa_mixed")
        s_oc_hi = sem("oc_hi")
        s_oc_mixed = sem("oc_mixed")
        s_stats = sem("stats")
        s_rstd = sem("rstd")
        s_rows = sem("rows")
        s_rows_used = sem("rows_used")
        s_hid_hi = sem("hid_hi")
        s_hid_ready = sem("hid_ready")
        s_mlp_evac = sem("mlp_evac")
        block = ctx.enter_context(nc.Block())

        def unit_source(layer, u):
            kind, c = CHUNKS[u // 4]
            r = 256 * (u % 4)
            if kind == "in":
                src = w_in[layer, r:r + 256, 512 * c:512 * c + 512]
            elif kind == "out":
                src = w_out[layer, r:r + 256, 512 * c:512 * c + 512]
            elif kind == "up":
                src = w_up[layer, r:r + 256, 512 * c:512 * c + 512]
            else:
                r += 1024 * (c // 2)
                src = w_down[layer, r:r + 256, 512 * (c % 2):512 * (c % 2) + 512]
            return src.rearrange("(k p) c -> p k c", p=P)

        @block.sync
        def _(sp):
            sp.dma_start(kc[:], consts[:, 0:K_END]).then_inc(s_const_in, 16)
            sp.dma_start(tmp[:, 0, 0:P], consts[:, K_MASK:K_MASK + P]).then_inc(s_const_in, 16)
            for tt in range(TT):
                sp.dma_start(xres[:, tt], x[0, tt * P:(tt + 1) * P, :]).then_inc(s_x_in, 16)

            def unit(layer, u):
                g = layer * UNITS + u
                if g >= RING:
                    sp.wait_ge(s_lo_ready, g - RING + 1)
                sp.dma_start(raw[:, u % RING].rearrange("p (k c) -> p k c", k=2), unit_source(layer, u)) \
                    .then_inc(s_raw[u % RING], 16)

            for layer in range(DEPTH):
                for u in range(RING):
                    unit(layer, u)
                if layer:
                    sp.wait_ge(s_x_normed, nth("x_normed", layer - 1, 2 * TT))
                else:
                    sp.wait_ge(s_blk_zero, 1)
                loads = [(gw_raw[:, :, :], w_in[layer, :, O_G:N_IN].rearrange("(k p) c -> p k c", p=P))]
                for n, a in enumerate((ln1_g, ln1_b, ln2_g, ln2_b)):
                    loads.append((ln_raw[8 * n:8 * n + 8, :], a[layer].rearrange("(k p) -> k p", p=P)))
                for n, a in enumerate((cmp_pe_k, cmp_pe_v)):
                    for dup in range(2):
                        loads.append((pe_raw[0:32, n, 64 * dup:64 * dup + 64], a[layer]))
                for n, a in enumerate((lam_q1, lam_k1, lam_q2, lam_k2)):
                    loads.append((lamv[:, n, :], a[layer:layer + 1, :].to_broadcast([P, 32])))
                for dup in range(2):
                    loads.append((subg[64 * dup:64 * dup + 64, 0:1], subln_g[layer].rearrange("(p a) -> p a", a=1)))
                for g in range(4):
                    r, c = 64 * (g % 2), g // 2
                    loads.append((w_blk[r:r + 64, c, r:r + 64], w_pool[layer, g]))
                loads.append((psc[:, :], pool_scale[layer].rearrange("(c p) -> p c", p=P)))
                for n, a in enumerate((w_cmp_k, w_cmp_v)):
                    loads.append((w_cmp[:, n].rearrange("p (j e) -> p j e", j=16),
                                  a[layer].rearrange("(j h) d e -> (h d) j e", h=2)))
                assert 16 * len(loads) == PER_LAYER["params"]
                for dst, src in loads:
                    sp.dma_start(dst, src, allow_slow_non_contiguous=True).then_inc(s_params, 16)
                for u in range(RING, UNITS):
                    unit(layer, u)
            for tt in range(TT):
                sp.wait_ge(s_out_normed, nth("out_normed", DEPTH - 1, tt + 1))
                sp.dma_start(out[0, tt * P:(tt + 1) * P, :], xres[:, tt]).then_inc(s_stored, 16)
            sp.wait_ge(s_stored, 16 * TT)

        @block.gpsimd
        def _(pool):
            chain = [0]

            def link(ins):
                ins.then_inc(s_chain_pool, 1)
                chain[0] += 1
                pool.wait_ge(s_chain_pool, chain[0])

            def split(layer, a, b):
                for u in range(a, b):
                    g = layer * UNITS + u
                    pool.wait_ge(s_hi_ready, nth("hi_ready", layer, u + 1))
                    if g >= RING:
                        pool.wait_ge(s_unit_used, g - RING + 1)
                    nc.gpsimd.tensor_tensor(w_lo[:, u % RING], raw[:, u % RING], w_hi[:, u % RING].bitcast(F32),
                                            ALU.subtract).then_inc(s_lo_ready, 1)

            def rstd_of(layer, ln):
                for tt in range(TT):
                    pool.wait_ge(s_stats, nth("stats", layer, TT * ln + tt + 1))
                    nc.gpsimd.tensor_tensor(rstd[:, tt:tt + 1], mv[:, tt, 1:2], kc[:, K_HALF:K_HALF + 1], ALU.pow) \
                        .then_inc(s_rstd, 1)

            nc.gpsimd.memset(w_blk[:], 0.0).then_inc(s_blk_zero, 1)
            for layer in range(DEPTH):
                split(layer, 0, U_OUT + RING)
                pool.wait_ge(s_turned, nth("turned", layer, Q_N))
                nc.gpsimd.memset(upad[:, :, 0:16], 0.0)
                nc.gpsimd.memset(boxb[:, :, 0:16], 0.0)
                link(nc.gpsimd.memset(boxc[:, 0:16], 0.0))
                pool.wait_ge(s_turned_dve, nth("turned_dve", layer, 4))
                pool.wait_ge(s_turned_act, nth("turned_act", layer, 5))
                w = slice(16, 16 + SEQ)

                def back(n):
                    return slice(16 - n, 16 + SEQ - n)

                for c in range(2):
                    b, u_ = boxb[:, c, :], upad[:, c, :]
                    add = nc.gpsimd.tensor_tensor
                    link(add(b[:, w], u_[:, w], u_[:, back(1)], ALU.add))
                    if c == 1:
                        link(add(boxc[:, w], b[:, w], b[:, back(2)], ALU.add))
                        link(add(b[:, w], boxc[:, w], boxc[:, back(4)], ALU.add))
                        link(add(boxc[64:P, w], b[64:P, w], b[64:P, back(8)], ALU.add))
                    else:
                        link(add(boxc[64:P, w], b[64:P, w], b[64:P, back(2)], ALU.add))
                    inv = kc[:, K_INV + c * SEQ:K_INV + (c + 1) * SEQ]
                    link(add(b[0:64, w], b[0:64, w], inv[0:64], ALU.mult))
                    link(add(b[64:P, w], boxc[64:P, w], inv[64:P], ALU.mult))
                    add(b[:, w], b[:, w], u_[:, w], ALU.subtract).then_inc(s_pool_y, 1)
                split(layer, U_OUT + RING, U_MLP + RING)
                rstd_of(layer, 0)
                split(layer, U_MLP + RING, UNITS)
                rstd_of(layer, 1)

        @block.tensor
        def _(pe):
            mm = nc.tensor.matmul

            def turn_x(layer, ln):
                for kt in range(KT):
                    for tt in range(TT):
                        last = nc.tensor.transpose(ps[:, kt, tt * P:(tt + 1) * P], xres[:, tt, kt * P:(kt + 1) * P], ident)
                    last.then_inc(s_xt_turned, 1)

            def gemm(layer, s, bank, a_hi, a_lo, ready):
                for q in range(4):
                    u = 4 * s + q
                    pe.wait_ge(s_lo_ready, nth("lo_ready", layer, u + 1))
                    pe.wait_ge(s_hi_ready, nth("hi_ready", layer, u + 1))
                    for k in (2 * q, 2 * q + 1):
                        ready(k)
                        first, end = k == 0, k == KT - 1
                        wh = w_hi[:, u % RING, 512 * (k % 2):512 * (k % 2) + 512]
                        wl = w_lo[:, u % RING, 512 * (k % 2):512 * (k % 2) + 512]
                        for b in range(4):
                            o, c = ps[:, bank + b, :], slice(b * P, (b + 1) * P)
                            if CHUNKS[s][0] == "up":
                                mm(o, wl[:, c], a_hi[:, k, :], start=first, stop=False)
                                mm(o, wh[:, c], a_hi[:, k, :], start=False, stop=False)
                                last = mm(o, wh[:, c], a_lo[:, k, :], start=False, stop=end)
                            else:
                                mm(o, a_lo[:, k, c], wh, start=first, stop=False)
                                mm(o, a_hi[:, k, c], wh, start=False, stop=False)
                                last = mm(o, a_hi[:, k, c], wl, start=False, stop=end)
                    last.then_inc(s_unit_used, 1)

            def scores(layer, t):
                if t >= 2:
                    pe.wait_ge(s_exped, nth("exped", layer, t - 1))
                h, i = (t // TT) % 6, t % TT
                n = P * (i + 1)
                for m in range(2):
                    if t < TASKS_A:
                        r, rl, qc, kq = 64 * (h % 2) + 32 * m, 32, h // 2, 3 + h // 2
                    else:
                        r, rl, qc, kq = 64 * (h // HG), 64, Q_QC - 2 + h % HG, Q_KSL - 2 + m
                    o = ps[:, 2 * (t % 2) + m, :]
                    mm(o[:, 0:n], qkt[r:r + rl, qc, i * P:n], qkt[r:r + rl, kq, 0:n], start=True, stop=False)
                    last = mm(o[:, i * P:n], ident16[:], mask16[:], start=False, stop=True)
                last.then_inc(s_scores, 1)

            def turn_p(layer, t):
                h, i = (t // TT) % 6, t % TT
                pe.wait_ge(s_probs, nth("probs", layer, t + 1))
                if t < TASKS_A:
                    if t >= 2:
                        pe.wait_ge(s_p_copied_act, nth("p_copied_act", layer, t - 1))
                    banks = (4 + t % 2,)
                else:
                    pe.wait_ge(s_p_copied_act, nth("p_copied_act", layer, t))
                    if t > TASKS_A:
                        pe.wait_ge(s_p_copied_dve, nth("p_copied_dve", layer, t - TASKS_A))
                    banks = (4, 5)
                for m, bank in enumerate(banks):
                    for j in range(i + 1):
                        last = nc.tensor.transpose(ps[:, bank, j * P:(j + 1) * P], probs[:, t % 2, m, j * P:(j + 1) * P], ident)
                last.then_inc(s_p_turned, 1)

            def values(layer, t):
                h, i = (t // TT) % 6, t % TT
                pe.wait_ge(s_p_copied_act, nth("p_copied_act", layer, t + 1))
                r, col = 64 * (h % 2), slice(i * P, (i + 1) * P)
                if t < TASKS_A:
                    if t % 8 == 0 and t:
                        pe.wait_ge(s_oa_squared, nth("oa_squared", layer, t // 8))
                    o = ps[r:r + 64, 6, col]
                    for j in range(i + 1):
                        last = mm(o, proj_v[:, j, V_A + 64 * h:V_A + 64 * h + 64], p_t[:, t % 2, 0, j * P:(j + 1) * P],
                                  start=j == 0, stop=j == i)
                else:
                    pe.wait_ge(s_p_copied_dve, nth("p_copied_dve", layer, t - TASKS_A + 1))
                    pair, g = h // 2, h // HG
                    if t == TASKS_A:
                        pe.wait_ge(s_oa_squared, nth("oa_squared", layer, 3))
                        pe.wait_ge(s_cmp_copied, nth("cmp_copied", layer, 1))
                    if pair == 1 and h == 2 and i == 0:
                        pe.wait_ge(s_ss_copied, nth("ss_copied", layer, 3))
                    if h == 4 and i == 0:
                        pe.wait_ge(s_oc_mixed, nth("oc_mixed", layer, 1))
                    o = ps[r:r + 64, 6 + pair % 2, col]
                    for j in range(i + 1):
                        for m, v in ((0, V_SL), (1, V_WI)):
                            mm(o, proj_v[:, j, v + 64 * g:v + 64 * g + 64], p_t[:, t % 2, m, j * P:(j + 1) * P],
                               start=j == 0 and m == 0, stop=False)
                    slot = 2 * (h % HG) + g
                    b = 32 * (slot % 4)
                    last = mm(o, vcmp[b:b + 32, :], cmp_pt[b:b + 32, i, slot // 4, :], start=False, stop=True)
                last.then_inc(s_pv, 1)

            pe.wait_ge(s_const_in, 32)
            for layer in range(DEPTH):
                if layer:
                    pe.wait_ge(s_x_normed, nth("x_normed", layer - 1, 2 * TT))
                else:
                    pe.wait_ge(s_x_in, 16 * TT)
                turn_x(layer, 0)
                for k, s in enumerate(range(5)):
                    if k >= 2:
                        pe.wait_ge(s_in_copied, nth("in_copied", layer, TT * (k - 1)))
                    if k == 1:
                        pe.wait_ge(s_params, nth("params", layer, PER_LAYER["params"]))
                        pe.wait_ge(s_xt_ready, nth("xt_ready", layer, KT))
                        nc.tensor.transpose(ps[:, 4, 0:32], ln_raw[0:32, :], ident[0:32, 0:32])
                        for n in range(2):
                            last = nc.tensor.transpose(ps[:, 4, 32 + 32 * n:64 + 32 * n], pe_raw[0:32, n, :], ident[0:32, 0:32])
                        last.then_inc(s_par_turned, 1)
                        pe.wait_ge(s_par_ready, nth("par_ready", layer, 1))
                    if k == 0:
                        pe.wait_ge(s_xt_ready, nth("xt_ready", layer, 4))
                    gemm(layer, s, 4 * (k % 2), xt_hi, xt_lo, lambda kt: pe.wait_ge(s_xt_ready, nth("xt_ready", layer, kt + 1)))
                pe.wait_ge(s_in_copied, nth("in_copied", layer, 4 * TT))
                pe.wait_ge(s_gw_lo, nth("gw_lo", layer, 1))
                for tt in range(TT):
                    o, c = ps[:, 4, 18 * tt:18 * tt + 18], slice(tt * P, (tt + 1) * P)
                    for k in range(KT):
                        mm(o, xt_lo[:, k, c], gw_hi[:, k, :], start=k == 0, stop=False)
                        mm(o, xt_hi[:, k, c], gw_hi[:, k, :], start=False, stop=False)
                        last = mm(o, xt_hi[:, k, c], gw_lo[:, k, :], start=False, stop=k == KT - 1)
                last.then_inc(s_gates_turned, 1)
                pe.wait_ge(s_in_copied, nth("in_copied", layer, 5 * TT))
                pe.wait_ge(s_exp_gates, nth("exp_gates", layer, 1))
                pe.wait_ge(s_roped_a, nth("roped_a", layer, TT))
                for q in range(Q_N):
                    if q == Q_QC:
                        pe.wait_ge(s_roped_c, nth("roped_c", layer, TT))
                    if q >= 8:
                        if q % 2:
                            pe.wait_ge(s_turned_dve, nth("turned_dve", layer, (q - 8) // 2 + 1))
                        else:
                            pe.wait_ge(s_turned_act, nth("turned_act", layer, (q - 8) // 2 + 1))
                    for tt in range(TT):
                        last = nc.tensor.transpose(ps[:, q % 8, tt * P:(tt + 1) * P], proj_t[:, tt, q * P:(q + 1) * P], ident)
                    last.then_inc(s_turned, 1)
                pe.wait_ge(s_turned_act, nth("turned_act", layer, 8))
                pe.wait_ge(s_turned_dve, nth("turned_dve", layer, 7))
                pe.wait_ge(s_cmp_rows, nth("cmp_rows", layer, 1))
                for n in range(2):
                    for j in range(16):
                        a, w = cmp_in[:, n, 64 * j:64 * j + 64], w_cmp[:, n, 64 * j:64 * j + 64]
                        st, wv = (w, a) if n == 0 else (a, w)
                        last = mm(ps[0:64, n, 0:64], st, wv, start=j == 0, stop=j == 15)
                last.then_inc(s_cmp_kv, 1)
                pe.wait_ge(s_cmp_kv_copied, nth("cmp_kv_copied", layer, 1))
                for g in range(2):
                    for i in range(TT):
                        for j in range(HG):
                            c = 32 * (HG * i + j)
                            last = mm(ps[:, 2 + g, c:c + 32], qkt[64 * g:64 * g + 64, Q_QC - 2 + j, i * P:(i + 1) * P],
                                      kcmp[64 * g:64 * g + 64, 32 * g:32 * g + 32], start=True, stop=True)
                last.then_inc(s_cmp_scores, 1)
                scores(layer, 0)
                pe.wait_ge(s_cmp_biased, nth("cmp_biased", layer, 1))
                scores(layer, 1)
                for t in range(TASKS):
                    if t == TASKS_A:
                        pe.wait_ge(s_cmp_probs, nth("cmp_probs", layer, 1))
                        pe.wait_ge(s_p_copied_act, nth("p_copied_act", layer, TASKS_A))
                        for i in range(TT):
                            for m, rl in ((0, P), (1, 64)):
                                c = 256 * (i % 2) + 128 * m
                                src = cmp_s[:, 6 * i + 4 * m:6 * i + 4 * m + rl // 32, :].rearrange("p s n -> p (s n)")
                                last = nc.tensor.transpose(ps[0:rl, 4 + i // 2, c:c + P], src, ident)
                        last.then_inc(s_cmp_turned, 1)
                        pe.wait_ge(s_cmp_copied, nth("cmp_copied", layer, 1))
                    if t + 2 < TASKS:
                        scores(layer, t + 2)
                    turn_p(layer, t)
                    if t >= 1:
                        values(layer, t - 1)
                    if t in (10, 18, 26):
                        pair = t // 8 - 1
                        pe.wait_ge(s_oa_squared, nth("oa_squared", layer, pair + 1))
                        if pair:
                            pe.wait_ge(s_ss_copied, nth("ss_copied", layer, pair))
                        if pair == 1:
                            pe.wait_ge(s_pool_scaled, nth("pool_scaled", layer, 2))
                        mm(ps[:, 7, :], blk_ones, rms[:, pair, :], start=True, stop=True).then_inc(s_ss_ready, 1)
                    if t in (12, 15):
                        c = (t - 12) // 3
                        pe.wait_ge(s_pool_y, nth("pool_y", layer, c + 1))
                        if c:
                            pe.wait_ge(s_pool_scaled, nth("pool_scaled", layer, 1))
                        else:
                            pe.wait_ge(s_ss_copied, nth("ss_copied", layer, 1))
                        mm(ps[:, 7, :], w_blk[:, c, :], boxb[:, c, 16:16 + SEQ], start=True, stop=True) \
                            .then_inc(s_pool_mm, 1)
                values(layer, TASKS - 1)
                def mixed(k):
                    if k == 0:
                        pe.wait_ge(s_oa_mixed, nth("oa_mixed", layer, 3))
                    elif k == 3:
                        pe.wait_ge(s_pool_mixed, nth("pool_mixed", layer, 2))
                    elif k >= 5:
                        pe.wait_ge(s_oc_mixed, nth("oc_mixed", layer, k - 4))
                pe.wait_ge(s_exped, nth("exped", layer, TASKS))
                for s in (5, 6):
                    if s == 6:
                        pe.wait_ge(s_p_copied_act, nth("p_copied_act", layer, TASKS))
                        pe.wait_ge(s_p_copied_dve, nth("p_copied_dve", layer, TASKS - TASKS_A))
                        pe.wait_ge(s_oc_mixed, nth("oc_mixed", layer, 3))
                    gemm(layer, s, 4 * (s - 5), mt_hi, mt_lo, mixed)
                pe.wait_ge(s_x_normed, nth("x_normed", layer, TT))
                turn_x(layer, 1)
                for k in range(N_MLP):
                    kind, c = MLP[k]
                    if k >= 2:
                        pe.wait_ge(s_mlp_evac, nth("mlp_evac", layer, 4 * (k - 1)))
                    if kind == "up":
                        if k == 0:
                            pe.wait_ge(s_xt_ready, nth("xt_ready", layer, KT + 4))
                        gemm(layer, 7 + k, 4 * (k % 2), xt_hi, xt_lo,
                             (lambda kt: pe.wait_ge(s_xt_ready, nth("xt_ready", layer, KT + kt + 1))) if k < 2 else (lambda kt: None))
                    else:
                        g = c // 2
                        a = (he_hi, he_lo) if g % 2 == 0 else (mt_hi, mt_lo)
                        gemm(layer, 7 + k, 4 * (k % 2), *a,
                             lambda kt: pe.wait_ge(s_hid_ready, nth("hid_ready", layer, 8 * g + kt + 1)))

        def place_turned(q):
            if Q_U <= q < Q_QC:
                return upad[:, q - Q_U, 16:16 + SEQ]
            return qkt[:, q if q < Q_U else q - 2, :]

        @block.scalar
        def _(act):
            A = nc.scalar.activation
            done = [0]

            def split_to(layer, end):
                for u in range(done[0], min(end, UNITS)):
                    g = layer * UNITS + u
                    act.wait_ge(s_raw[u % RING], nth("raw", layer, 16 * (u // RING + 1)))
                    if g >= RING:
                        act.wait_ge(s_unit_used, g - RING + 1)
                    A(w_hi[:, u % RING], raw[:, u % RING], ACT.Copy).then_inc(s_hi_ready, 1)
                done[0] = max(done[0], min(end, UNITS))

            def scale_x(layer, ln):
                gi = 2 if ln == 0 else 0
                for kt in range(KT):
                    s = KT * ln + kt
                    act.wait_ge(s_xt_turned, nth("xt_turned", layer, s + 1))
                    if kt >= 2:
                        act.wait_ge(s_xt_ready, nth("xt_ready", layer, s - 1))
                    A(tmp[:, kt % 2], ps[:, kt, :], ACT.Identity, scale=lnp[:, gi, kt:kt + 1],
                      bias=lnp[:, gi + 1, kt:kt + 1]).then_inc(s_xt_scaled, 1)

            def copy_in(layer, k, b):
                c0 = 512 * IN_ORDER[k]
                cuts = []
                for o, n, turn, to in PIECES:
                    lo, hi = max(o, c0), min(o + n, c0 + 512)
                    if lo < hi:
                        cuts.append((lo - c0, hi - lo, turn, to + lo - o))
                for n, (c, width, turn, to) in enumerate(cuts):
                    kept = proj_t if turn else proj_v
                    last = A(kept[:, b, to:to + width], ps[:, 4 * (k % 2) + b, c:c + width], ACT.Copy)
                last.then_inc(s_in_copied, 1)

            act.wait_ge(s_masks, 1)
            for layer in range(DEPTH):
                done[0] = 0
                split_to(layer, RING)
                scale_x(layer, 0)
                act.wait_ge(s_params, nth("params", layer, PER_LAYER["params"]))
                A(gw_hi[:], gw_raw[:], ACT.Copy).then_inc(s_gw_hi, 1)
                for n in range(1, U_OUT):
                    if n == 4:
                        act.wait_ge(s_par_turned, nth("par_turned", layer, 1))
                        A(lnp[:].rearrange("p a k -> p (a k)"), ps[:, 4, 0:32], ACT.Copy)
                        A(pe_t[:].rearrange("p a l -> p (a l)"), ps[:, 4, 32:96], ACT.Copy).then_inc(s_par_ready, 1)
                    split_to(layer, n + RING)
                    if n >= 4:
                        act.wait_ge(s_unit_used, nth("unit_used", layer, n // 4 * 4))
                        copy_in(layer, n // 4 - 1, n % 4)
                split_to(layer, U_OUT + RING)
                act.wait_ge(s_unit_used, nth("unit_used", layer, U_OUT))
                for b in range(TT):
                    copy_in(layer, 4, b)
                act.wait_ge(s_gates_turned, nth("gates_turned", layer, 1))
                A(gates[:].rearrange("p a g -> p (a g)"), ps[:, 4, 0:TT * GATES], ACT.Exp, scale=-1.0) \
                    .then_inc(s_exp_gates, 1)
                act.wait_ge(s_lam_dot, nth("lam_dot", layer, 1))
                A(lams[:, 2:4], lams[:, 0:2], ACT.Exp).then_inc(s_lam_exp, 1)
                for q in range(0, Q_N, 2):
                    act.wait_ge(s_turned, nth("turned", layer, q + 1))
                    A(place_turned(q), ps[:, q % 8, :], ACT.Copy).then_inc(s_turned_act, 1)
                act.wait_ge(s_cmp_kv, nth("cmp_kv", layer, 1))
                for half in range(2):
                    A(kcmp[64 * half:64 * half + 64, :], ps[0:64, 0, 0:64], ACT.Copy)
                    last = A(vcmp[64 * half:64 * half + 64, :], ps[0:64, 1, 0:64], ACT.Copy)
                last.then_inc(s_cmp_kv_copied, 1)

                def exps(t):
                    n = P * (t % TT + 1)
                    act.wait_ge(s_negmax, nth("negmax", layer, t + 1))
                    if t >= 2:
                        act.wait_ge(s_p_turned, nth("p_turned", layer, t - 1))
                    for m in range(2):
                        last = A(probs[:, t % 2, m, 0:n], ps[:, 2 * (t % 2) + m, 0:n], ACT.Exp,
                                 bias=negmax[:, t % 4, m:m + 1], accum_out=sums[:, t % 4, m:m + 1])
                    last.then_inc(s_exped, 1)

                def copy_p(t):
                    n = P * (t % TT + 1)
                    act.wait_ge(s_p_turned, nth("p_turned", layer, t + 1))
                    if t >= 2:
                        act.wait_ge(s_pv, nth("pv", layer, t - 1))
                    A(p_t[:, t % 2, 0, 0:n], ps[:, 4 + (t % 2 if t < TASKS_A else 0), 0:n], ACT.Copy) \
                        .then_inc(s_p_copied_act, 1)

                def oc_high(pair):
                    act.wait_ge(s_pv, nth("pv", layer, TASKS_A + 8 * pair + 8))
                    A(mt_hi[:, 5 + pair], ps[:, 6 + pair % 2, :], ACT.Copy).then_inc(s_oc_hi, 1)

                for t in range(TASKS):
                    exps(t)
                    if t == 2:
                        act.wait_ge(s_cmp_shifted, nth("cmp_shifted", layer, 1))
                        flat = cmp_s[:].rearrange("p s n -> p (s n)")
                        A(flat, flat, ACT.Exp).then_inc(s_cmp_exp, 1)
                    if t:
                        copy_p(t - 1)
                    if t == TASKS_A:
                        act.wait_ge(s_cmp_turned, nth("cmp_turned", layer, 1))
                        for half in range(2):
                            src = ps[:, 4 + half, :].rearrange("p (i m q) -> p i m q", i=2, m=2)
                            A(cmp_pt[:, 2 * half:2 * half + 2, 0, :], src[:, :, 0, :], ACT.Copy)
                            last = A(cmp_pt[0:64, 2 * half:2 * half + 2, 1, :], src[0:64, :, 1, :], ACT.Copy)
                        last.then_inc(s_cmp_copied, 1)
                    if t in (9, 17, 25):
                        pair = t // 8 - 1
                        act.wait_ge(s_pv, nth("pv", layer, 8 * pair + 8))
                        A(oa[:, pair], ps[:, 6, :], ACT.Copy).then_inc(s_oa_copied, 1)
                        A(rms[:, pair], ps[:, 6, :], ACT.Square).then_inc(s_oa_squared, 1)
                    if t in (14, 17):
                        c = (t - 14) // 3
                        act.wait_ge(s_pool_scaled, nth("pool_scaled", layer, c + 1))
                        A(mt_hi[:, 3 + c], boxb[:, c, 16:16 + SEQ], ACT.Copy).then_inc(s_pool_hi, 1)
                    if t in (33, 41):
                        oc_high(t // 8 - 4)
                copy_p(TASKS - 1)
                oc_high(2)
                act.wait_ge(s_ss_copied, nth("ss_copied", layer, 3))
                flat = rms[:].rearrange("p a q -> p (a q)")
                A(flat, flat, ACT.Ln).then_inc(s_chain_act, 1)
                act.wait_ge(s_chain_act, layer + 1)
                A(flat, flat, ACT.Exp, scale=-0.5).then_inc(s_rms_ready, 1)
                for pair in range(3):
                    act.wait_ge(s_oa_normed, nth("oa_normed", layer, pair + 1))
                    A(mt_hi[:, pair], oa[:, pair], ACT.Copy).then_inc(s_oa_hi, 1)
                act.wait_ge(s_oa_mixed, nth("oa_mixed", layer, 3))
                for n, a in enumerate((ln1_g, ln1_b)):
                    act.dma_start(rows[:, n], a[layer:layer + 1, :].to_broadcast([P, D])).then_inc(s_rows, 16)
                for n in range(U_OUT, U_MLP):
                    split_to(layer, n + RING)
                split_to(layer, U_MLP + RING)
                scale_x(layer, 1)
                for k in range(N_MLP):
                    if k == 2:
                        act.wait_ge(s_rows_used, nth("rows_used", layer, 1))
                        for n, a in enumerate((ln2_g, ln2_b)):
                            act.dma_start(rows[:, n], a[layer:layer + 1, :].to_broadcast([P, D])).then_inc(s_rows, 16)
                    kind, c = MLP[k - 1] if k else ("", 0)
                    for b in range(4):
                        split_to(layer, U_MLP + 4 * k + b + RING)
                        if kind == "up":
                            g, f = c // 2, 4 * (c % 2) + b
                            if g >= 2 and f == 0:
                                used = U_MLP + 4 * (MLP.index(("down", 2 * (g - 2) + 1)) + 1)
                                act.wait_ge(s_unit_used, nth("unit_used", layer, used))
                            act.wait_ge(s_mlp_evac, nth("mlp_evac", layer, 4 * (k - 1) + b + 1))
                            A((mt_hi if g % 2 else he_hi)[:, f], tmp[:, f % 2], ACT.Copy).then_inc(s_hid_hi, 1)

        @block.vector
        def _(dve):
            V = nc.vector
            chain = [0]

            def link(ins):
                ins.then_inc(s_chain_dve, 1)
                chain[0] += 1
                dve.wait_ge(s_chain_dve, chain[0])

            def split_x(layer, ln):
                for kt in range(KT):
                    s = KT * ln + kt
                    dve.wait_ge(s_xt_scaled, nth("xt_scaled", layer, s + 1))
                    link(V.tensor_copy(xt_hi[:, kt], tmp[:, kt % 2]))
                    V.tensor_tensor(xt_lo[:, kt], tmp[:, kt % 2], xt_hi[:, kt].bitcast(F32), ALU.subtract) \
                        .then_inc(s_xt_ready, 1)

            def affine_rows(layer, ln):
                dve.wait_ge(s_rows, nth("rows", layer, 32 * (ln + 1)))
                for tt in range(TT):
                    link(V.tensor_tensor(xres[:, tt], xres[:, tt], rows[:, 0], ALU.mult))
                    last = V.tensor_tensor(xres[:, tt], xres[:, tt], rows[:, 1], ALU.add)
                    if ln:
                        last.then_inc(s_out_normed, 1)
                    elif tt == TT - 1:
                        last.then_inc(s_rows_used, 1)

            def rotate(tt, parts):
                flat = tmp[:].rearrange("p a c -> p (a c)")
                base = parts[0][0]
                k = K_ROPE + ROPE_W * tt
                for col, heads, dim, _, sc in parts:
                    w, half = heads * dim, dim // 2
                    xv = proj_t[:, tt, col:col + w].rearrange("p (h a d) -> p h a d", a=2, d=half)
                    tv = flat[:, col - base:col - base + w].rearrange("p (h a d) -> p h a d", a=2, d=half)
                    for a in range(2):
                        s = kc[:, k + sc + a * half:k + sc + (a + 1) * half].unsqueeze(1).to_broadcast([P, heads, half])
                        last = V.tensor_tensor(tv[:, :, a, :], xv[:, :, 1 - a, :], s, ALU.mult)
                link(last)
                for col, heads, dim, cc, _ in parts:
                    w, half = heads * dim, dim // 2
                    c = kc[:, k + cc:k + cc + half].unsqueeze(1).to_broadcast([P, 2 * heads, half])
                    xf = proj_t[:, tt, col:col + w].rearrange("p (h d) -> p h d", d=half)
                    last = V.tensor_tensor(xf, xf, c, ALU.mult)
                link(last)
                total = sum(h * d for _, h, d, _, _ in parts)
                whole = proj_t[:, tt, base:base + total]
                return V.tensor_tensor(whole, whole, flat[:, 0:total], ALU.add)

            def half_stats(tt, half):
                return V.bn_stats(bst[:, tt, half, :], xres[:, tt, 512 * half:512 * half + 512])

            def normalise(layer, ln, tt):
                dve.wait_ge(s_rstd, nth("rstd", layer, TT * ln + tt + 1))
                V.tensor_scalar(xres[:, tt], xres[:, tt], mv[:, tt, 0:1], rstd[:, tt:tt + 1], ALU.subtract, ALU.mult) \
                    .then_inc(s_x_normed, 1)

            def finish_rows(layer, ln, add):
                for tt in range(TT):
                    add(tt)
                    link(half_stats(tt, 1))
                    link(V.bn_aggr(mv[:, tt, :], bst[:, tt].rearrange("p a s -> p (a s)")))
                    V.tensor_scalar(mv[:, tt, 1:2], mv[:, tt, 1:2], LN_EPS, None, ALU.add).then_inc(s_stats, 1)
                    if tt:
                        normalise(layer, ln, tt - 1)
                normalise(layer, ln, TT - 1)

            dve.wait_ge(s_const_in, 32)
            V.tensor_copy(ident16[:], ident)
            V.tensor_copy(mask16[:], tmp[:, 0, 0:P])
            V.memset(lnp[:, 2, :], 1.0)
            V.memset(lnp[:, 3, :], 0.0).then_inc(s_masks, 1)
            for layer in range(DEPTH):
                split_x(layer, 0)
                if layer:
                    dve.wait_ge(s_xt_turned, nth("xt_turned", layer, KT))
                    affine_rows(layer - 1, 1)
                dve.wait_ge(s_gw_hi, nth("gw_hi", layer, 1))
                V.tensor_tensor(gw_lo[:], gw_raw[:], gw_hi[:].bitcast(F32), ALU.subtract).then_inc(s_gw_lo, 1)
                prod = bst[:].rearrange("p a b c -> p (a b c)")[:, 0:32]
                link(V.tensor_tensor(prod, lamv[:, 0], lamv[:, 1], ALU.mult))
                link(V.tensor_reduce(lams[:, 0:1], prod, AX.X, ALU.add))
                link(V.tensor_tensor(prod, lamv[:, 2], lamv[:, 3], ALU.mult))
                V.tensor_reduce(lams[:, 1:2], prod, AX.X, ALU.add) \
                    .then_inc(s_lam_dot, 1)
                V.tensor_scalar(subg[:, 1:2], subg[:, 0:1], kc[:, K_LAM + 2 * layer + 1:K_LAM + 2 * layer + 2], None, ALU.mult)
                dve.wait_ge(s_in_copied, nth("in_copied", layer, 2 * TT))
                for tt in range(TT):
                    rotate(tt, ((T_QA, 12, 32, R_CAQ, R_SAQ), (T_KA, 12, 32, R_CAK, R_SAK))).then_inc(s_roped_a, 1)
                    dve.wait_ge(s_roped_a, nth("roped_a", layer, tt + 1))
                dve.wait_ge(s_in_copied, nth("in_copied", layer, 4 * TT))
                for tt in range(TT):
                    link(rotate(tt, ((T_KCM, 6, 64, R_CCK, R_SCK),)))
                for tt in range(TT):
                    dve.wait_ge(s_in_copied, nth("in_copied", layer, 4 * TT + tt + 1))
                    rotate(tt, ((T_QC, 6, 64, R_CCQ, R_SCQ),)).then_inc(s_roped_c, 1)
                    dve.wait_ge(s_roped_c, nth("roped_c", layer, tt + 1))
                dve.wait_ge(s_exp_gates, nth("exp_gates", layer, 1))
                link(V.tensor_scalar(gates[:], gates[:], 1.0, None, ALU.add))
                link(V.reciprocal(gates[:], gates[:]))
                dve.wait_ge(s_lam_exp, nth("lam_exp", layer, 1))
                link(V.tensor_tensor(lams[:, 4:5], lams[:, 3:4], lams[:, 2:3], ALU.subtract))
                link(V.tensor_tensor(lams[:, 5:6], lams[:, 4:5], kc[:, K_LAM + 2 * layer:K_LAM + 2 * layer + 1], ALU.subtract))
                for q in range(1, Q_N, 2):
                    dve.wait_ge(s_turned, nth("turned", layer, q + 1))
                    V.tensor_copy(place_turned(q), ps[:, q % 8, :]).then_inc(s_turned_dve, 1)
                dve.wait_ge(s_turned, nth("turned", layer, Q_N))
                dve.wait_ge(s_turned_act, nth("turned_act", layer, 7))
                pad = cmp_in[:].rearrange("p a (c n) -> p a c n", n=32)
                V.memset(pad[:, :, :, 31:32], 0.0)
                for kv, q in ((0, Q_KCM - 2), (1, Q_VCM)):
                    for g in range(2):
                        r = slice(64 * g, 64 * g + 64)
                        for h in range(2):
                            for jh in range(2):
                                src = qkt[r, q, :].rearrange("p (n j h) -> p h j n", j=8, h=2)[:, h, :, jh:jh + 31]
                                pos = pe_t[r, kv, :].rearrange("p (a j h) -> p h a j", a=2, h=2)[:, h, jh, :]
                                dst = cmp_in[64 * h:64 * h + 64, kv].rearrange("p (j g n) -> p g j n", g=2, n=32)
                                last = V.tensor_tensor(dst[:, g, 8 * jh:8 * jh + 8, 0:31], src,
                                                       pos.unsqueeze(2).to_broadcast([64, 8, 31]), ALU.add)
                last.then_inc(s_cmp_rows, 1)
                dve.wait_ge(s_cmp_scores, nth("cmp_scores", layer, 1))
                sv = cmp_s[:].rearrange("p (i j g) n -> p g i j n", i=TT, j=HG)
                for g in range(2):
                    cb = kc[:, K_CB:K_CB + TT * 32].rearrange("p (i n) -> p i n", i=TT).unsqueeze(2) \
                        .to_broadcast([P, TT, HG, 32])
                    src = ps[:, 2 + g, 0:TT * HG * 32].rearrange("p (i j n) -> p i j n", i=TT, j=HG)
                    last = V.tensor_tensor(sv[:, g], src, cb, ALU.add)
                last.then_inc(s_cmp_biased, 1)
                dve.wait_ge(s_cmp_biased, nth("cmp_biased", layer, 1))

                def negative_max(t):
                    n = P * (t % TT + 1)
                    dve.wait_ge(s_scores, nth("scores", layer, t + 1))
                    b = 2 * (t % 2)
                    V.tensor_reduce(negmax[:, t % 4, :], ps[:, b:b + 2, 0:n], AX.X, ALU.max, negate=True) \
                        .then_inc(s_negmax, 1)

                def over24(a):
                    return cst[:, a, :].unsqueeze(2).to_broadcast([P, TT * 6, 32])

                link(V.tensor_reduce(cst[:, 0, :], cmp_s[:], AX.X, ALU.max))
                V.tensor_tensor(cmp_s[:], cmp_s[:], over24(0), ALU.subtract).then_inc(s_cmp_shifted, 1)

                def weights(t):
                    h, i = (t // TT) % 6, t % TT
                    n, s = P * (i + 1), t % 4
                    dve.wait_ge(s_exped, nth("exped", layer, t + 1))
                    p0, p1 = probs[:, t % 2, 0, 0:n], probs[:, t % 2, 1, 0:n]
                    link(V.reciprocal(recs[:, s, :], sums[:, s, :]))
                    if t < TASKS_A:
                        V.tensor_tensor(facs[:, s, 0:1], recs[:, s, 1:2], lams[:, 5:6], ALU.mult)
                        link(V.tensor_scalar(p0, p0, recs[:, s, 0:1], None, ALU.mult))
                        last = V.scalar_tensor_tensor(p0, p1, facs[:, s, 0:1], p0, ALU.mult, ALU.add)
                    else:
                        link(V.tensor_tensor(facs[:, s, :], recs[:, s, :], gates[:, i, 3 * h + 1:3 * h + 3], ALU.mult))
                        V.tensor_scalar(p0, p0, facs[:, s, 0:1], None, ALU.mult)
                        last = V.tensor_scalar(p1, p1, facs[:, s, 1:2], None, ALU.mult)
                    last.then_inc(s_probs, 1)

                def copy_p(t):
                    n = P * (t % TT + 1)
                    dve.wait_ge(s_p_turned, nth("p_turned", layer, t + 1))
                    dve.wait_ge(s_pv, nth("pv", layer, t - 1))
                    V.tensor_copy(p_t[:, t % 2, 1, 0:n], ps[:, 5, 0:n]).then_inc(s_p_copied_dve, 1)

                def oc_low(pair):
                    dve.wait_ge(s_oc_hi, nth("oc_hi", layer, pair + 1))
                    V.tensor_tensor(mt_lo[:, 5 + pair], ps[:, 6 + pair % 2, :], mt_hi[:, 5 + pair].bitcast(F32),
                                    ALU.subtract).then_inc(s_oc_mixed, 1)

                negative_max(0)
                for t in range(TASKS):
                    if t + 1 < TASKS:
                        negative_max(t + 1)
                    weights(t)
                    if t > TASKS_A:
                        copy_p(t - 1)
                    if t == 4:
                        dve.wait_ge(s_cmp_exp, nth("cmp_exp", layer, 1))
                        link(V.tensor_reduce(cst[:, 1, :], cmp_s[:], AX.X, ALU.add))
                        link(V.reciprocal(cst[:, 2, :], cst[:, 1, :]))
                        gv = gates[:].rearrange("p i (g j r) -> p i j g r", g=2, r=3)[:, :, :, :, 0]
                        fv = cst[:, 2, :].rearrange("p (i j g) -> p i j g", i=TT, j=HG)
                        ov = cst[:, 3, :].rearrange("p (i j g) -> p i j g", i=TT, j=HG)
                        V.tensor_tensor(ov, fv, gv, ALU.mult)
                        cm = kc[:, K_CM:K_CM + TT * 32].rearrange("p (i n) -> p i n", i=TT).unsqueeze(2) \
                            .to_broadcast([P, TT, 6, 32])
                        cv = cmp_s[:].rearrange("p (i s) n -> p i s n", i=TT)
                        link(V.tensor_tensor(cv, cv, cm, ALU.mult))
                        V.tensor_tensor(cmp_s[:], cmp_s[:], over24(3), ALU.mult).then_inc(s_cmp_probs, 1)
                    if t in (11, 19, 27):
                        pair = t // 8 - 1
                        dve.wait_ge(s_ss_ready, nth("ss_ready", layer, pair + 1))
                        V.tensor_scalar(rms[:, pair], ps[:, 7, :], 1.0 / DV, RMS_EPS, ALU.mult, ALU.add) \
                            .then_inc(s_ss_copied, 1)
                    if t in (13, 16):
                        c = (t - 13) // 3
                        dve.wait_ge(s_pool_mm, nth("pool_mm", layer, c + 1))
                        V.tensor_scalar(boxb[:, c, 16:16 + SEQ], ps[:, 7, :], psc[:, c:c + 1], None, ALU.mult) \
                            .then_inc(s_pool_scaled, 1)
                    if t in (15, 18):
                        c = (t - 15) // 3
                        dve.wait_ge(s_pool_hi, nth("pool_hi", layer, c + 1))
                        V.tensor_tensor(mt_lo[:, 3 + c], boxb[:, c, 16:16 + SEQ], mt_hi[:, 3 + c].bitcast(F32),
                                        ALU.subtract).then_inc(s_pool_mixed, 1)
                    if t in (34, 42):
                        oc_low(t // 8 - 4)
                copy_p(TASKS - 1)
                oc_low(2)
                dve.wait_ge(s_rms_ready, nth("rms_ready", layer, 1))
                for pair in range(3):
                    V.scalar_tensor_tensor(oa[:, pair], oa[:, pair], subg[:, 1:2], rms[:, pair], ALU.mult, ALU.mult) \
                        .then_inc(s_oa_normed, 1)
                for pair in range(3):
                    dve.wait_ge(s_oa_hi, nth("oa_hi", layer, pair + 1))
                    V.tensor_tensor(mt_lo[:, pair], oa[:, pair], mt_hi[:, pair].bitcast(F32), ALU.subtract) \
                        .then_inc(s_oa_mixed, 1)
                def add_bank(tt, half, bank, alpha):
                    xs = xres[:, tt, 512 * half:512 * half + 512]
                    if alpha:
                        return V.scalar_tensor_tensor(xs, xs, ALPHA, ps[:, bank + tt, :], ALU.mult, ALU.add)
                    return V.tensor_tensor(xs, xs, ps[:, bank + tt, :], ALU.add)

                dve.wait_ge(s_unit_used, nth("unit_used", layer, U_OUT + 4))
                for tt in range(TT):
                    link(add_bank(tt, 0, 0, True))
                    half_stats(tt, 0)
                dve.wait_ge(s_unit_used, nth("unit_used", layer, U_OUT + 8))
                finish_rows(layer, 0, lambda tt: link(add_bank(tt, 1, 4, True)))
                split_x(layer, 1)
                dve.wait_ge(s_xt_turned, nth("xt_turned", layer, 2 * KT))
                affine_rows(layer, 0)
                for k, (kind, c) in enumerate(MLP):
                    bank = 4 * (k % 2)
                    dve.wait_ge(s_unit_used, nth("unit_used", layer, U_MLP + 4 * (k + 1)))
                    if kind == "up":
                        g = c // 2
                        hi, lo = (mt_hi, mt_lo) if g % 2 else (he_hi, he_lo)

                        def low(b):
                            f = 4 * (c % 2) + b
                            dve.wait_ge(s_hid_hi, nth("hid_hi", layer, 4 * c + b + 1))
                            V.tensor_tensor(lo[:, f], tmp[:, f % 2], hi[:, f].bitcast(F32), ALU.subtract) \
                                .then_inc(s_hid_ready, 1)

                        for b in range(4):
                            f = 4 * (c % 2) + b
                            if 4 * c + b >= 2:
                                dve.wait_ge(s_hid_ready, nth("hid_ready", layer, 4 * c + b - 1))
                            link(V.tensor_scalar(tmp[:, f % 2], ps[:, bank + b, :], 0.0, None, ALU.max))
                            V.tensor_tensor(tmp[:, f % 2], tmp[:, f % 2], ps[:, bank + b, :], ALU.mult) \
                                .then_inc(s_mlp_evac, 1)
                            if b:
                                low(b - 1)
                        low(3)
                    else:
                        g, half = c // 2, c % 2

                        def add(tt):
                            add_bank(tt, half, bank, g == 0).then_inc(s_mlp_evac, 1)
                            dve.wait_ge(s_mlp_evac, nth("mlp_evac", layer, 4 * k + tt + 1))

                        if k < N_MLP - 1:
                            for tt in range(TT):
                                add(tt)
                                if k == N_MLP - 2:
                                    half_stats(tt, 0)
                        else:
                            finish_rows(layer, 1, add)
            affine_rows(DEPTH - 1, 1)


INPUTS = ("x", "w_in", "lam_q1", "lam_k1", "lam_q2", "lam_k2", "subln_g", "w_pool", "pool_scale", "cmp_pe_k",
          "cmp_pe_v", "w_cmp_k", "w_cmp_v", "w_out", "ln1_g", "ln1_b", "w_up", "w_down", "ln2_g", "ln2_b")


def kernel(**inputs):
    import concourse.bacc as bacc
    from concourse.bass_utils import run_bass_kernel_spmd

    nc = bacc.Bacc("TRN2", target_bir_lowering=False, num_devices=1)
    arrays, args = {}, []
    for name in INPUTS + ("consts",):
        a = np.ascontiguousarray(shape_constants() if name == "consts" else inputs[name])
        arrays[f"in_{name}"] = a
        args.append(nc.dram_tensor(f"in_{name}", a.shape, mybir.dt.from_np(a.dtype), kind="ExternalInput").ap())
    args.append(nc.dram_tensor("out_x", (1, SEQ, D), F32, kind="ExternalOutput").ap())
    build(nc, *args)
    r = run_bass_kernel_spmd(nc, [arrays], core_ids=[0])
    return r.results[0]["out_x"]
```

```python
from contextlib import ExitStack

import numpy as np

from concourse import mybir

F32 = mybir.dt.float32
F32R = mybir.dt.float32r
BF16 = mybir.dt.bfloat16
ALU = mybir.AluOpType
ACT = mybir.ActivationFunctionType
AX = mybir.AxisListType

P = 128
SEQ, D, DEPTH, DFF = 512, 1024, 2, 4096
TT = SEQ // P
KT = D // P
A_HEADS, A_DQ, DV = 6, 32, 64
C_HEADS, HG = 6, 3
N_IN = 2578
GATES = 18
WINDOWS = (2, 4, 8, 16)
N_CMP, CMP_L = 31, 32
ALPHA = (2 * DEPTH) ** 0.25
LN_EPS, RMS_EPS = 1e-5, 1e-6
A_SCALE, C_SCALE = A_DQ ** -0.5, 64 ** -0.5
NEG = -1.0e30

O_VA, O_U, O_QC, O_KCM, O_VCM, O_KSL, O_VSL, O_KWI, O_VWI, O_G = (
    768, 1152, 1408, 1792, 1920, 2048, 2176, 2304, 2432, 2560)
T_QA, T_KA, T_VCM, T_U, T_QC, T_KCM, T_KSL, T_KWI, T_END = 0, 384, 768, 896, 1152, 1536, 1664, 1792, 1920
V_A, V_SL, V_WI, V_END = 0, 384, 512, 640
PIECES = ((0, 768, True, T_QA), (O_VA, 384, False, V_A), (O_U, 256, True, T_U),
          *((O_QC + 64 * h, 64, True, T_QC + 128 * (h % HG) + 64 * (h // HG)) for h in range(C_HEADS)),
          (O_KCM, 128, True, T_KCM), (O_VCM, 128, True, T_VCM), (O_KSL, 128, True, T_KSL),
          (O_VSL, 128, False, V_SL), (O_KWI, 128, True, T_KWI), (O_VWI, 128, False, V_WI))
Q_KA, Q_VCM, Q_U, Q_QC, Q_KCM, Q_KSL, Q_KWI = 3, 6, 7, 9, 12, 13, 14
S_QA, S_VCM, S_QC, S_KCM, S_KSL, S_KWI, S_N = 0, 3, 4, 7, 8, 10, 12
TURN_A = ((0, 4), (3, 5), (1, 6), (5, 2), (2, 3), (4, 7))
N_MLP = 16
MLP = (("up", 0), ("up", 1), ("up", 2), ("up", 3), ("down", 0), ("down", 1), ("up", 4), ("up", 5),
       ("down", 2), ("down", 3), ("up", 6), ("up", 7), ("down", 4), ("down", 5), ("down", 6), ("down", 7))
U_IN, U_OUT, U_MLP = 0, 20, 28
UNITS = U_MLP + 4 * N_MLP
RING = 4
TURN_BANK = (4, 0)
TASKS_A = A_HEADS * TT
TASKS = TASKS_A + C_HEADS * TT
SIDE = {0: ("turn", 6), 1: ("turn", 12), 2: ("turn", 7), 3: ("turn", 8), 4: ("turn", 9), 5: ("turn", 10),
        6: ("turn", 11), 7: ("compress", 0), 8: ("turn", 13), 9: ("turn", 14), 10: ("cmp_scores", 0),
        11: ("cmp_scores", 1), 12: ("square_sums", 0), 13: ("gates", 0), 16: ("cmp_turn", 0), 17: ("cmp_turn", 1),
        19: ("square_sums", 1), 22: ("pool", 0), 23: ("pool", 1), 26: ("square_sums", 2)}
SIDE_NUMBER = {step: n for n, step in enumerate(SIDE)}

K_ID, K_BLK = 0, 128
K_ROPE = 256
ROPE_W = 16 + 32 + 16 + 32 + 32 + 64 + 32 + 64
R_CAQ, R_SAQ, R_CAK, R_SAK, R_CCK, R_SCK, R_CCQ, R_SCQ = 0, 16, 48, 64, 96, 128, 192, 224
K_INV = K_ROPE + TT * ROPE_W
K_CM = K_INV + 2 * SEQ
K_CB = K_CM + TT * 32
K_LAM = K_CB + TT * 32
K_HALF = K_LAM + 2 * DEPTH
K_ROWS = K_HALF + 1
K_END = K_ROWS + 6
K_MASK = K_END


def shape_constants():
    k = np.zeros((P, K_MASK + P), np.float32)
    p = np.arange(P)
    k[:, K_ID:K_ID + P] = np.eye(P)
    k[:, K_BLK:K_BLK + P] = (p[:, None] // 64 == p[None, :] // 64)
    k[:, K_MASK:K_MASK + P] = np.where(p[None, :] > p[:, None], NEG, 0.0)
    t = (np.arange(TT)[None, :] * P + p[:, None])

    def table(dim):
        inv = np.float32(1.0) / np.float32(10000.0) ** (np.arange(0, dim, 2, dtype=np.float32) / np.float32(dim))
        ang = np.arange(SEQ, dtype=np.float32)[:, None] * inv[None, :].astype(np.float32)
        c, s = np.cos(ang)[t], np.sin(ang)[t]
        return c, np.concatenate([-s, s], -1)

    (ca, sa), (cc, sc) = table(A_DQ), table(64)
    rope = np.concatenate([ca * A_SCALE, sa * A_SCALE, ca, sa, cc, sc, cc * C_SCALE, sc * C_SCALE], -1)
    k[:, K_ROPE:K_INV] = rope.reshape(P, -1)
    tt = np.arange(SEQ)
    for c in range(2):
        for half in range(2):
            cnt = np.minimum(tt + 1, WINDOWS[2 * c + half])
            k[64 * half:64 * half + 64, K_INV + c * SEQ:K_INV + (c + 1) * SEQ] = 1.0 / cnt
    n = np.arange(32)
    seen = (n[None, None, :] < N_CMP) & (16 * n[None, None, :] + 31 <= t[:, :, None])
    k[:, K_CM:K_CB] = seen.reshape(P, -1)
    k[:, K_CB:K_LAM] = np.where(seen, 0.0, NEG).reshape(P, -1)
    for l in range(DEPTH):
        lam_init = 0.8 - 0.6 * np.exp(-0.3 * l)
        k[:, K_LAM + 2 * l] = lam_init
        k[:, K_LAM + 2 * l + 1] = 1.0 - lam_init
    k[:, K_HALF] = -0.5
    k[:, K_ROWS:K_ROWS + 4] = (p[:, None] // 32 == np.arange(4))
    k[:, K_ROWS + 4:K_ROWS + 6] = (p[:, None] // 64 == np.arange(2))
    return k


PER_LAYER = dict(
    raw=16 * UNITS // RING,
    hi_ready=UNITS, lo_ready=UNITS, unit_used=UNITS,
    x_normed=2 * TT, out_normed=TT, xt_turned=2 * KT, xt_scaled=2 * KT, xt_ready=2 * KT,
    params=16 * 21, value_weights=16, par_turned=1, par_ready=1, gw_hi=1, gw_lo=1, lam_dot=1, lam_exp=1,
    in_copied=5 * TT, roped_a=TT, roped_c=TT, roped_k=TT, gates_done=1, exp_gates=1, bank_done=2 * 3,
    turned=6, turned_act=2, turned_dve=4, side_ready=len(SIDE), side_emptied=len(SIDE), kcmp_zero=1,
    cmp_rows=1, cmp_shifted=1, cmp_exp=1, cmp_probs=1,
    pool_y=2, pool_hi=2, pool_mixed=2,
    scores=TASKS, negmax=TASKS, exped=TASKS, probs=TASKS, p_turned=TASKS, p_copied=TASKS,
    pv=TASKS,
    oa_copied=3, oa_squared=3, rms_ready=1, oa_normed=3, oa_hi=3, oa_mixed=3,
    oc_hi=3, oc_mixed=3,
    stats=2 * TT, rstd=2 * TT, rows=64, rows_used=1, hid_hi=32, hid_ready=32, mlp_evac=4 * N_MLP,
)

CHUNKS = [("in", c) for c in range(5)] + [("out", 0), ("out", 1)] + list(MLP)


def build(nc, x, w_in, lam_q1, lam_k1, lam_q2, lam_k2, subln_g, w_pool, pool_scale, cmp_pe_k, cmp_pe_v,
          w_cmp_k, w_cmp_v, w_out, ln1_g, ln1_b, w_up, w_down, ln2_g, ln2_b, consts, out):
    ctx = ExitStack()
    with ctx:
        top = [16512]

        def at(name, offset, shape, dt=F32):
            return nc.alloc_sbuf_tensor_at(name, [P] + list(shape), dt, offset=offset)

        def room(nbytes):
            top[0] += nbytes
            return top[0] - nbytes

        def sb(name, shape, dt=F32):
            size = int(np.prod(shape)) * (2 if dt == BF16 else 4)
            return at(name, room((size + 31) // 32 * 32), shape, dt)

        kc = sb("kc", [K_END])
        ident = kc[:, K_ID:K_ID + P]
        blk_ones = kc[:, K_BLK:K_BLK + P]
        ident16 = sb("ident16", [P], BF16)
        mask16 = sb("mask16", [P], BF16)
        xres = sb("xres", [TT, D])
        raw = sb("raw", [RING, 1024])
        w_hi = sb("w_hi", [RING, 1024], F32R)
        w_lo = sb("w_lo", [RING, 1024], F32R)
        ra = room(32768)
        xt_hi, xt_lo = at("xt_hi", ra, [KT, SEQ], F32R), at("xt_lo", ra + 16384, [KT, SEQ], F32R)
        qkt, upad = at("qkt", ra, [S_N, SEQ]), at("upad", ra + 2048 * S_N, [2, 16 + SEQ])
        boxc = at("boxc", ra + 28800, [16 + SEQ])
        rb = room(32768)
        mt_hi, mt_lo = at("mt_hi", rb, [KT, SEQ], F32R), at("mt_lo", rb + 16384, [KT, SEQ], F32R)
        ka_slots = at("ka_slots", rb, [2 * KT, SEQ])
        boxb = at("boxb", rb + 3 * 2048, [2, 16 + SEQ])
        rc = room(32768)
        he_hi, he_lo = at("he_hi", rc, [KT, SEQ], F32R), at("he_lo", rc + 16384, [KT, SEQ], F32R)
        proj_a = at("proj_a", rc, [TT, T_VCM])
        proj_b = at("proj_b", rc + 12288, [TT, T_END - T_VCM])
        probs = at("probs", rc, [2, 2, SEQ])
        p_t = at("p_t", rc + 8192, [2, 2, SEQ])
        cmp_s = at("cmp_s", rc + 16384, [TT * 6, 32])
        cmp_pt = at("cmp_pt", rc + 19456, [TT, 2, P])
        pooled = at("pooled", rc + 24576, [2, SEQ])
        gates_t = at("gates_t", rc + 30720, [SEQ])
        proj_v = sb("proj_v", [TT, V_END])
        rd = room(12288)
        oa, rms = at("oa", rd, [3, SEQ]), at("rms", rd + 6144, [3, SEQ])
        cmp_kw = at("cmp_kw", rd, [16, 2, 64])
        rows, tmp = at("rows", rd, [2, D]), at("tmp", rd + 8192, [2, 512])
        cmp_wv = sb("cmp_wv", [16, 2, 64])
        w_blk = sb("w_blk", [2, P])
        gw_raw, gw_hi, gw_lo = sb("gw_raw", [KT, GATES]), sb("gw_hi", [KT, GATES], F32R), sb("gw_lo", [KT, GATES], F32R)
        ln_raw = sb("ln_raw", [P])
        pe_raw = sb("pe_raw", [2, 2 * 64])
        lnp = sb("lnp", [4, KT])
        pe_t = sb("pe_t", [2, 32])
        lamv = sb("lamv", [4, 32])
        lams = sb("lams", [8])
        subg = sb("subg", [2])
        psc = sb("psc", [2])
        gates = sb("gates", [TT, GATES])
        kcmp, vcmp = sb("kcmp", [64]), sb("vcmp", [64])
        bst, mv = sb("bst", [TT, 2, 6]), sb("mv", [TT, 2])
        rstd = sb("rstd", [TT])
        negmax, sums, recs, facs = (sb(n, [4, 2]) for n in ("negmax", "sums", "recs", "facs"))
        cst = sb("cst", [4, TT * 6])
        assert top[0] <= 229368, top[0]
        ps = ctx.enter_context(nc.psum_tensor("ps", [P, 8, 512], F32))

        def ka_slot(h, m):
            n = 2 * h + m
            return ka_slots[:, n if n < 3 else n + 3, :]

        def turned_source(q, tt):
            kept, col = (proj_a, q * P) if q < Q_VCM else (proj_b, q * P - T_VCM)
            return kept[:, tt, col:col + P]

        def sem(name):
            return ctx.enter_context(nc.semaphore(name))

        def nth(name, layer, n):
            return layer * PER_LAYER[name] + n

        s_raw = [sem(f"raw{r}") for r in range(RING)]
        s_ident_in = sem("ident_in")
        s_const_in = sem("const_in")
        s_x_in = sem("x_in")
        s_masks = sem("masks")
        s_ones = sem("ones")
        s_blk_zero = sem("blk_zero")
        s_chain_dve = sem("chain_dve")
        s_chain_act = sem("chain_act")
        s_chain_pool = sem("chain_pool")
        s_stored = sem("stored")
        s_hi_ready = sem("hi_ready")
        s_lo_ready = sem("lo_ready")
        s_unit_used = sem("unit_used")
        s_x_normed = sem("x_normed")
        s_out_normed = sem("out_normed")
        s_xt_turned = sem("xt_turned")
        s_xt_scaled = sem("xt_scaled")
        s_xt_ready = sem("xt_ready")
        s_params = sem("params")
        s_par_turned = sem("par_turned")
        s_par_ready = sem("par_ready")
        s_gw_hi = sem("gw_hi")
        s_gw_lo = sem("gw_lo")
        s_lam_dot = sem("lam_dot")
        s_lam_exp = sem("lam_exp")
        s_in_copied = sem("in_copied")
        s_roped_a = sem("roped_a")
        s_roped_c = sem("roped_c")
        s_roped_k = sem("roped_k")
        s_bank_done = sem("bank_done")
        s_gates_done = sem("gates_done")
        s_exp_gates = sem("exp_gates")
        s_turned = sem("turned")
        s_turned_act = sem("turned_act")
        s_turned_dve = sem("turned_dve")
        s_cmp_rows = sem("cmp_rows")
        s_cmp_shifted = sem("cmp_shifted")
        s_cmp_exp = sem("cmp_exp")
        s_cmp_probs = sem("cmp_probs")
        s_side_ready = sem("side_ready")
        s_side_emptied = sem("side_emptied")
        s_kcmp_zero = sem("kcmp_zero")
        s_value_weights = sem("value_weights")
        s_pool_y = sem("pool_y")
        s_pool_hi = sem("pool_hi")
        s_pool_mixed = sem("pool_mixed")
        s_scores = sem("scores")
        s_negmax = sem("negmax")
        s_exped = sem("exped")
        s_probs = sem("probs")
        s_p_turned = sem("p_turned")
        s_p_copied = sem("p_copied")
        s_pv = sem("pv")
        s_oa_copied = sem("oa_copied")
        s_oa_squared = sem("oa_squared")
        s_rms_ready = sem("rms_ready")
        s_oa_normed = sem("oa_normed")
        s_oa_hi = sem("oa_hi")
        s_oa_mixed = sem("oa_mixed")
        s_oc_hi = sem("oc_hi")
        s_oc_mixed = sem("oc_mixed")
        s_stats = sem("stats")
        s_rstd = sem("rstd")
        s_rows = sem("rows")
        s_rows_used = sem("rows_used")
        s_hid_hi = sem("hid_hi")
        s_hid_ready = sem("hid_ready")
        s_mlp_evac = sem("mlp_evac")
        block = ctx.enter_context(nc.Block())

        def unit_source(layer, u):
            kind, c = CHUNKS[u // 4]
            r = 256 * (u % 4)
            if kind == "in":
                src = w_in[layer, r:r + 256, 512 * c:512 * c + 512]
            elif kind == "out":
                src = w_out[layer, r:r + 256, 512 * c:512 * c + 512]
            elif kind == "up":
                src = w_up[layer, r:r + 256, 512 * c:512 * c + 512]
            else:
                r += 1024 * (c // 2)
                src = w_down[layer, r:r + 256, 512 * (c % 2):512 * (c % 2) + 512]
            return src.rearrange("(k p) c -> p k c", p=P)

        def rotate(tensor_tensor, link, tt, parts):
            flat = tmp[:].rearrange("p a c -> p (a c)")
            base = parts[0][0]
            kept, off = (proj_a, 0) if base < T_VCM else (proj_b, T_VCM)
            k = K_ROPE + ROPE_W * tt
            for col, heads, dim, _, sc in parts:
                w, half = heads * dim, dim // 2
                xv = kept[:, tt, col - off:col - off + w].rearrange("p (h a d) -> p h a d", a=2, d=half)
                tv = flat[:, col - base:col - base + w].rearrange("p (h a d) -> p h a d", a=2, d=half)
                for a in range(2):
                    s = kc[:, k + sc + a * half:k + sc + (a + 1) * half].unsqueeze(1).to_broadcast([P, heads, half])
                    last = tensor_tensor(tv[:, :, a, :], xv[:, :, 1 - a, :], s, ALU.mult)
            link(last)
            for col, heads, dim, cc, _ in parts:
                w, half = heads * dim, dim // 2
                c = kc[:, k + cc:k + cc + half].unsqueeze(1).to_broadcast([P, 2 * heads, half])
                xf = kept[:, tt, col - off:col - off + w].rearrange("p (h d) -> p h d", d=half)
                last = tensor_tensor(xf, xf, c, ALU.mult)
            link(last)
            total = sum(h * d for _, h, d, _, _ in parts)
            whole = kept[:, tt, base - off:base - off + total]
            return tensor_tensor(whole, whole, flat[:, 0:total], ALU.add)

        @block.sync
        def _(sp):
            sp.dma_start(ident, consts[:, K_ID:K_ID + P]).then_inc(s_ident_in, 16)
            for tt in range(TT):
                sp.dma_start(xres[:, tt], x[0, tt * P:(tt + 1) * P, :]).then_inc(s_x_in, 16)

            def unit(layer, u):
                g = layer * UNITS + u
                if g >= RING:
                    sp.wait_ge(s_lo_ready, g - RING + 1)
                sp.dma_start(raw[:, u % RING].rearrange("p (k c) -> p k c", k=2), unit_source(layer, u)) \
                    .then_inc(s_raw[u % RING], 16)

            for layer in range(DEPTH):
                for u in range(RING):
                    unit(layer, u)
                if layer:
                    sp.wait_ge(s_x_normed, nth("x_normed", layer - 1, 2 * TT))
                else:
                    sp.dma_start(kc[:, P:K_END], consts[:, P:K_END]).then_inc(s_const_in, 16)
                    sp.dma_start(rows[:, 0, 0:P], consts[:, K_MASK:K_MASK + P]).then_inc(s_const_in, 16)
                    sp.wait_ge(s_blk_zero, 1)
                loads = [(gw_raw[:, :, :], w_in[layer, :, O_G:N_IN].rearrange("(k p) c -> p k c", p=P))]
                for n, a in enumerate((ln1_g, ln1_b, ln2_g, ln2_b)):
                    loads.append((ln_raw[8 * n:8 * n + 8, :], a[layer].rearrange("(k p) -> k p", p=P)))
                for n, a in enumerate((cmp_pe_k, cmp_pe_v)):
                    for dup in range(2):
                        loads.append((pe_raw[0:32, n, 64 * dup:64 * dup + 64], a[layer]))
                for n, a in enumerate((lam_q1, lam_k1, lam_q2, lam_k2)):
                    loads.append((lamv[:, n, :], a[layer:layer + 1, :].to_broadcast([P, 32])))
                for dup in range(2):
                    loads.append((subg[64 * dup:64 * dup + 64, 0:1], subln_g[layer].rearrange("(p a) -> p a", a=1)))
                for g in range(4):
                    r, c = 64 * (g % 2), g // 2
                    loads.append((w_blk[r:r + 64, c, r:r + 64], w_pool[layer, g]))
                loads.append((psc[:, :], pool_scale[layer].rearrange("(c p) -> p c", p=P)))
                loads.append((cmp_wv[:, :, 0, :], w_cmp_k[layer].rearrange("(j h) d e -> (h d) j e", h=2)))
                assert 16 * len(loads) == PER_LAYER["params"]
                for dst, src in loads:
                    sp.dma_start(dst, src, allow_slow_non_contiguous=True).then_inc(s_params, 16)
                for u in range(RING, UNITS):
                    if u == 3 * RING:
                        if layer:
                            sp.wait_ge(s_out_normed, nth("out_normed", layer - 1, TT))
                        else:
                            sp.wait_ge(s_masks, 1)
                        sp.dma_start(cmp_kw[:, :, 1, :], w_cmp_v[layer].rearrange("(j h) d e -> (h d) j e", h=2)) \
                            .then_inc(s_value_weights, 16)
                    unit(layer, u)
            for tt in range(TT):
                sp.wait_ge(s_out_normed, nth("out_normed", DEPTH - 1, tt + 1))
                sp.dma_start(out[0, tt * P:(tt + 1) * P, :], xres[:, tt]).then_inc(s_stored, 16)
            sp.wait_ge(s_stored, 16 * TT)

        @block.gpsimd
        def _(pool):
            chain = [0]

            def link(ins):
                ins.then_inc(s_chain_pool, 1)
                chain[0] += 1
                pool.wait_ge(s_chain_pool, chain[0])

            def split(layer, a, b):
                for u in range(a, b):
                    g = layer * UNITS + u
                    pool.wait_ge(s_hi_ready, nth("hi_ready", layer, u + 1))
                    if g >= RING:
                        pool.wait_ge(s_unit_used, g - RING + 1)
                    nc.gpsimd.tensor_tensor(w_lo[:, u % RING], raw[:, u % RING], w_hi[:, u % RING].bitcast(F32),
                                            ALU.subtract).then_inc(s_lo_ready, 1)

            def rstd_of(layer, ln):
                for tt in range(TT):
                    pool.wait_ge(s_stats, nth("stats", layer, TT * ln + tt + 1))
                    nc.gpsimd.tensor_tensor(rstd[:, tt:tt + 1], mv[:, tt, 1:2], kc[:, K_HALF:K_HALF + 1], ALU.pow) \
                        .then_inc(s_rstd, 1)

            def rows_to_compress(kv):
                to, part = (cmp_kw, 0) if kv == 0 else (cmp_wv, 1)
                pad = to[:, :, part, :].rearrange("p j (g n) -> p j g n", n=32)
                link(nc.gpsimd.memset(pad[:, :, :, 31:32], 0.0))
                for g in range(2):
                    r = slice(64 * g, 64 * g + 64)
                    for h in range(2):
                        for jh in range(2):
                            src = qkt[r, S_KCM if kv == 0 else S_VCM, :] \
                                .rearrange("p (n j h) -> p h j n", j=8, h=2)[:, h, :, jh:jh + 31]
                            pos = pe_t[r, kv, :].rearrange("p (a j h) -> p h a j", a=2, h=2)[:, h, jh, :]
                            if (g, h, jh) != (0, 0, 0):
                                link(last)
                            last = nc.gpsimd.tensor_tensor(pad[64 * h:64 * h + 64, 8 * jh:8 * jh + 8, g, 0:31], src,
                                                   pos.unsqueeze(2).to_broadcast([64, 8, 31]), ALU.add)
                return last

            nc.gpsimd.memset(w_blk[:], 0.0).then_inc(s_blk_zero, 1)
            for layer in range(DEPTH):
                split(layer, 0, U_OUT + RING)
                pool.wait_ge(s_const_in, 32)
                pool.wait_ge(s_side_emptied, nth("side_emptied", layer, 1))
                pool.wait_ge(s_value_weights, nth("value_weights", layer, 16))
                link(rows_to_compress(1))
                pool.wait_ge(s_side_emptied, nth("side_emptied", layer, 2))
                rows_to_compress(0).then_inc(s_cmp_rows, 1)
                pool.wait_ge(s_cmp_rows, nth("cmp_rows", layer, 1))
                for tt in range(TT):
                    rotate(nc.gpsimd.tensor_tensor, link, tt, ((T_KSL, 4, 64, R_CCK, R_SCK),)).then_inc(s_roped_k, 1)
                    pool.wait_ge(s_roped_k, nth("roped_k", layer, tt + 1))
                pool.wait_ge(s_side_emptied, nth("side_emptied", layer, 4))
                nc.gpsimd.memset(upad[:, :, 0:16], 0.0)
                nc.gpsimd.memset(boxb[:, :, 0:16], 0.0)
                link(nc.gpsimd.memset(boxc[:, 0:16], 0.0))
                w = slice(16, 16 + SEQ)

                def back(n):
                    return slice(16 - n, 16 + SEQ - n)

                for c in range(2):
                    b, u_ = boxb[:, c, :], upad[:, c, :]
                    add = nc.gpsimd.tensor_tensor
                    link(add(b[:, w], u_[:, w], u_[:, back(1)], ALU.add))
                    if c == 1:
                        link(add(boxc[:, w], b[:, w], b[:, back(2)], ALU.add))
                        link(add(b[:, w], boxc[:, w], boxc[:, back(4)], ALU.add))
                        link(add(boxc[64:P, w], b[64:P, w], b[64:P, back(8)], ALU.add))
                    else:
                        link(add(boxc[64:P, w], b[64:P, w], b[64:P, back(2)], ALU.add))
                    inv = kc[:, K_INV + c * SEQ:K_INV + (c + 1) * SEQ]
                    link(add(b[0:64, w], b[0:64, w], inv[0:64], ALU.mult))
                    link(add(b[64:P, w], boxc[64:P, w], inv[64:P], ALU.mult))
                    add(b[:, w], b[:, w], u_[:, w], ALU.subtract).then_inc(s_pool_y, 1)
                split(layer, U_OUT + RING, U_MLP + RING)
                rstd_of(layer, 0)
                split(layer, U_MLP + RING, UNITS)
                rstd_of(layer, 1)

        @block.tensor
        def _(pe):
            mm = nc.tensor.matmul

            def turn_x(layer, ln, kt, tt):
                t = nc.tensor.transpose(ps[:, TURN_BANK[ln] + kt % 4, tt * P:(tt + 1) * P], xres[:, tt, kt * P:(kt + 1) * P], ident)
                if tt == TT - 1:
                    t.then_inc(s_xt_turned, 1)

            def turned_ahead(layer, ln, k):
                if 1 <= k <= 4:
                    for tt in range(TT):
                        turn_x(layer, ln, k + 3, tt)
                pe.wait_ge(s_xt_ready, nth("xt_ready", layer, KT * ln + k + 1))

            def gemm(layer, s, bank, a_hi, a_lo, ready, units=range(4), by_bank=False):
                def products(k, b):
                    first, end = k == 0, k == KT - 1
                    u = 4 * s + k // 2
                    wh = w_hi[:, u % RING, 512 * (k % 2):512 * (k % 2) + 512]
                    wl = w_lo[:, u % RING, 512 * (k % 2):512 * (k % 2) + 512]
                    o, c = ps[:, bank + b, :], slice(b * P, (b + 1) * P)
                    if CHUNKS[s][0] == "up":
                        mm(o, wl[:, c], a_hi[:, k, :], start=first, stop=False)
                        mm(o, wh[:, c], a_hi[:, k, :], start=False, stop=False)
                        return mm(o, wh[:, c], a_lo[:, k, :], start=False, stop=end)
                    mm(o, a_lo[:, k, c], wh, start=first, stop=False)
                    mm(o, a_hi[:, k, c], wh, start=False, stop=False)
                    return mm(o, a_hi[:, k, c], wl, start=False, stop=end)

                for q in units:
                    u = 4 * s + q
                    pe.wait_ge(s_lo_ready, nth("lo_ready", layer, u + 1))
                    pe.wait_ge(s_hi_ready, nth("hi_ready", layer, u + 1))
                    for k in (2 * q, 2 * q + 1):
                        ready(k)
                        if not (by_bank and q >= 2):
                            for b in range(4):
                                last = products(k, b)
                    if not (by_bank and q >= 2):
                        last.then_inc(s_unit_used, 1)
                if by_bank:
                    for b in range(4):
                        for k in range(4, KT):
                            last = products(k, b)
                            if b == 3 and k % 2:
                                last.then_inc(s_unit_used, 1)
                        if b < 3:
                            last.then_inc(s_bank_done, 1)

            def scores(layer, t):
                if t >= 2:
                    pe.wait_ge(s_exped, nth("exped", layer, t - 1))
                h, i = (t // TT) % 6, t % TT
                n = P * (i + 1)
                for m in range(2):
                    if t < TASKS_A:
                        queries, keys = qkt[:, S_QA + h // 2, i * P:n], ka_slot(h, m)
                    else:
                        queries, keys = qkt[:, S_QC + h % HG, i * P:n], qkt[:, S_KSL + 2 * m + h // HG, :]
                    o = ps[:, 2 * (t % 2) + m, :]
                    mm(o[:, 0:n], queries, keys[:, 0:n], start=True, stop=False)
                    last = mm(o[:, i * P:n], ident16[:], mask16[:], start=False, stop=True)
                last.then_inc(s_scores, 1)

            def turn_p(layer, t):
                h, i = (t // TT) % 6, t % TT
                pe.wait_ge(s_probs, nth("probs", layer, t + 1))
                if t < TASKS_A:
                    if t >= 2:
                        pe.wait_ge(s_p_copied, nth("p_copied", layer, t - 1))
                    banks = (4 + t % 2,)
                else:
                    pe.wait_ge(s_p_copied, nth("p_copied", layer, t))
                    banks = (4, 5)
                for m, bank in enumerate(banks):
                    for j in range(i + 1):
                        last = nc.tensor.transpose(ps[:, bank, j * P:(j + 1) * P], probs[:, t % 2, m, j * P:(j + 1) * P], ident)
                last.then_inc(s_p_turned, 1)

            def values(layer, t):
                h, i = (t // TT) % 6, t % TT
                pe.wait_ge(s_p_copied, nth("p_copied", layer, t + 1))
                r, col = 64 * (h % 2), slice(i * P, (i + 1) * P)
                if t < TASKS_A:
                    if t % 8 == 0 and t:
                        pe.wait_ge(s_oa_squared, nth("oa_squared", layer, t // 8))
                    o = ps[r:r + 64, 6, col]
                    for j in range(i + 1):
                        last = mm(o, proj_v[:, j, V_A + 64 * h:V_A + 64 * h + 64], p_t[:, 0, t % 2, j * P:(j + 1) * P],
                                  start=j == 0, stop=j == i)
                else:
                    pair, g = h // 2, h // HG
                    if t == TASKS_A:
                        pe.wait_ge(s_oa_squared, nth("oa_squared", layer, 3))
                    if h == 2 and i == 0:
                        pe.wait_ge(s_side_emptied, nth("side_emptied", layer, len(SIDE)))
                    if h == 4 and i == 0:
                        pe.wait_ge(s_oc_mixed, nth("oc_mixed", layer, 1))
                    o = ps[r:r + 64, 6 + pair % 2, col]
                    for j in range(i + 1):
                        for m, v in ((0, V_SL), (1, V_WI)):
                            mm(o, proj_v[:, j, v + 64 * g:v + 64 * g + 64], p_t[:, m, t % 2, j * P:(j + 1) * P],
                               start=j == 0 and m == 0, stop=False)
                    slot = 2 * (h % HG) + g
                    b = 32 * (slot % 4)
                    last = mm(o, vcmp[b:b + 32, :], cmp_pt[b:b + 32, i, slot // 4, :], start=False, stop=True)
                last.then_inc(s_pv, 1)

            def side(layer, t):
                n, (kind, c) = SIDE_NUMBER[t], SIDE[t]
                if n:
                    pe.wait_ge(s_side_emptied, nth("side_emptied", layer, n))
                else:
                    pe.wait_ge(s_turned_dve, nth("turned_dve", layer, 4))
                    pe.wait_ge(s_turned_act, nth("turned_act", layer, 2))
                if kind == "turn":
                    if Q_QC <= c <= Q_KCM:
                        pe.wait_ge(s_roped_c, nth("roped_c", layer, TT))
                    elif c > Q_KCM:
                        pe.wait_ge(s_roped_k, nth("roped_k", layer, TT))
                    for tt in range(TT):
                        last = nc.tensor.transpose(ps[:, 7, tt * P:(tt + 1) * P], turned_source(c, tt), ident)
                elif kind == "compress":
                    pe.wait_ge(s_value_weights, nth("value_weights", layer, 16))
                    pe.wait_ge(s_cmp_rows, nth("cmp_rows", layer, 1))
                    for j in range(16):
                        last = mm(ps[:, 7, 0:P], cmp_wv[:, j].rearrange("p a e -> p (a e)"),
                                  cmp_kw[:, j].rearrange("p a e -> p (a e)"), start=j == 0, stop=j == 15)
                elif kind == "cmp_scores":
                    for i in range(2):
                        for j in range(HG):
                            o = 64 * (HG * i + j)
                            last = mm(ps[:, 7, o:o + 64], qkt[:, S_QC + j, (2 * c + i) * P:(2 * c + i + 1) * P], kcmp[:],
                                      start=True, stop=True)
                elif kind == "gates":
                    for tt in range(TT):
                        last = nc.tensor.transpose(ps[:, 7, GATES * tt:GATES * (tt + 1)], gates_t[0:GATES, tt * P:(tt + 1) * P],
                                                   ident[0:GATES, 0:GATES])
                elif kind == "square_sums":
                    pe.wait_ge(s_oa_squared, nth("oa_squared", layer, c + 1))
                    last = mm(ps[:, 7, :], blk_ones, rms[:, c, :], start=True, stop=True)
                elif kind == "pool":
                    pe.wait_ge(s_pool_y, nth("pool_y", layer, c + 1))
                    last = mm(ps[:, 7, :], w_blk[:, c, :], boxb[:, c, 16:16 + SEQ], start=True, stop=True)
                else:
                    pe.wait_ge(s_cmp_probs, nth("cmp_probs", layer, 1))
                    for i in range(2):
                        for m, rl in ((0, P), (1, 64)):
                            o, s = 256 * i + 128 * m, 6 * (2 * c + i) + 4 * m
                            src = cmp_s[:, s:s + rl // 32, :].rearrange("p s n -> p (s n)")
                            last = nc.tensor.transpose(ps[0:rl, 7, o:o + P], src, ident)
                last.then_inc(s_side_ready, 1)

            pe.wait_ge(s_ident_in, 16)
            for layer in range(DEPTH):
                for tt in range(TT):
                    if layer:
                        pe.wait_ge(s_x_normed, nth("x_normed", layer - 1, TT + tt + 1))
                    else:
                        pe.wait_ge(s_x_in, 16 * TT)
                    for kt in range(4):
                        turn_x(layer, 0, kt, tt)
                for k, s in enumerate(range(5)):
                    if k >= 2:
                        pe.wait_ge(s_in_copied, nth("in_copied", layer, TT * (k - 1)))
                    if k == 1:
                        pe.wait_ge(s_params, nth("params", layer, PER_LAYER["params"]))
                        pe.wait_ge(s_xt_ready, nth("xt_ready", layer, KT))
                        nc.tensor.transpose(ps[:, 4, 0:32], ln_raw[0:32, :], ident[0:32, 0:32])
                        for n in range(2):
                            last = nc.tensor.transpose(ps[:, 4, 32 + 32 * n:64 + 32 * n], pe_raw[0:32, n, :], ident[0:32, 0:32])
                        last.then_inc(s_par_turned, 1)
                        pe.wait_ge(s_par_ready, nth("par_ready", layer, 1))
                    gemm(layer, s, 4 * (k % 2), xt_hi, xt_lo,
                         (lambda kt: turned_ahead(layer, 0, kt)) if k == 0 else (lambda kt: None))
                pe.wait_ge(s_in_copied, nth("in_copied", layer, 4 * TT))
                pe.wait_ge(s_gw_lo, nth("gw_lo", layer, 1))
                for k in range(KT):
                    o = ps[0:GATES, 7, :]
                    mm(o, gw_hi[:, k, :], xt_lo[:, k, :], start=k == 0, stop=False)
                    mm(o, gw_hi[:, k, :], xt_hi[:, k, :], start=False, stop=False)
                    last = mm(o, gw_lo[:, k, :], xt_hi[:, k, :], start=False, stop=k == KT - 1)
                last.then_inc(s_gates_done, 1)
                pe.wait_ge(s_roped_a, nth("roped_a", layer, TT))
                for n, (q, bank) in enumerate(TURN_A):
                    if n == 3:
                        pe.wait_ge(s_in_copied, nth("in_copied", layer, 5 * TT))
                    if bank == 7:
                        pe.wait_ge(s_exp_gates, nth("exp_gates", layer, 1))
                    for tt in range(TT):
                        last = nc.tensor.transpose(ps[:, bank, tt * P:(tt + 1) * P], turned_source(q, tt), ident)
                    last.then_inc(s_turned, 1)
                pe.wait_ge(s_masks, 1)
                pe.wait_ge(s_turned_dve, nth("turned_dve", layer, 1))
                pe.wait_ge(s_turned_act, nth("turned_act", layer, 1))
                scores(layer, 0)
                pe.wait_ge(s_turned_dve, nth("turned_dve", layer, 3))
                pe.wait_ge(s_turned_act, nth("turned_act", layer, 2))
                scores(layer, 1)
                def mixed(k):
                    if k == 0:
                        pe.wait_ge(s_oa_mixed, nth("oa_mixed", layer, 3))
                    elif k == 3:
                        pe.wait_ge(s_pool_mixed, nth("pool_mixed", layer, 2))
                    elif k >= 5:
                        pe.wait_ge(s_oc_mixed, nth("oc_mixed", layer, k - 4))

                for t in range(TASKS):
                    if t + 2 < TASKS:
                        scores(layer, t + 2)
                    if t == TASKS - 1:
                        pe.wait_ge(s_exped, nth("exped", layer, TASKS))
                        gemm(layer, 5, 0, mt_hi, mt_lo, mixed, (0,))
                    turn_p(layer, t)
                    if t >= 1:
                        values(layer, t - 1)
                    if t in SIDE:
                        side(layer, t)
                gemm(layer, 5, 0, mt_hi, mt_lo, mixed, (1,))
                values(layer, TASKS - 1)
                gemm(layer, 5, 0, mt_hi, mt_lo, mixed, (2, 3))
                gemm(layer, 6, 4, mt_hi, mt_lo, mixed, by_bank=True)
                for tt in range(TT):
                    pe.wait_ge(s_x_normed, nth("x_normed", layer, tt + 1))
                    for kt in range(4):
                        turn_x(layer, 1, kt, tt)
                for k in range(N_MLP):
                    kind, c = MLP[k]
                    if k >= 2:
                        pe.wait_ge(s_mlp_evac, nth("mlp_evac", layer, 4 * (k - 1)))
                    if kind == "up":
                        gemm(layer, 7 + k, 4 * ((k + 1) % 2), xt_hi, xt_lo,
                             (lambda kt: turned_ahead(layer, 1, kt)) if k == 0 else (lambda kt: None))
                    else:
                        g = c // 2
                        a = (he_hi, he_lo) if g % 2 == 0 else (mt_hi, mt_lo)
                        gemm(layer, 7 + k, 4 * ((k + 1) % 2), *a,
                             lambda kt: pe.wait_ge(s_hid_ready, nth("hid_ready", layer, 8 * g + kt + 1)), by_bank=k == N_MLP - 1)

        @block.scalar
        def _(act):
            A = nc.scalar.activation
            done = [0]

            def split_to(layer, end):
                for u in range(done[0], min(end, UNITS)):
                    g = layer * UNITS + u
                    act.wait_ge(s_raw[u % RING], nth("raw", layer, 16 * (u // RING + 1)))
                    if g >= RING:
                        act.wait_ge(s_unit_used, g - RING + 1)
                    A(w_hi[:, u % RING], raw[:, u % RING], ACT.Copy).then_inc(s_hi_ready, 1)
                done[0] = max(done[0], min(end, UNITS))

            def scale_x(layer, ln):
                gi = 2 if ln == 0 else 0
                for kt in range(KT):
                    s = KT * ln + kt
                    act.wait_ge(s_xt_turned, nth("xt_turned", layer, s + 1))
                    if kt >= 2:
                        act.wait_ge(s_xt_ready, nth("xt_ready", layer, s - 1))
                    A(tmp[:, kt % 2], ps[:, TURN_BANK[ln] + kt % 4, :], ACT.Identity, scale=lnp[:, gi, kt:kt + 1],
                      bias=lnp[:, gi + 1, kt:kt + 1]).then_inc(s_xt_scaled, 1)

            def copy_in(layer, k, b):
                c0 = 512 * k
                cuts = []
                for o, n, turn, to in PIECES:
                    lo, hi = max(o, c0), min(o + n, c0 + 512)
                    if lo < hi:
                        cuts.append((lo - c0, hi - lo, turn, to + lo - o))
                for n, (c, width, turn, to) in enumerate(cuts):
                    kept = proj_v if not turn else proj_a if to < T_VCM else proj_b
                    to -= T_VCM if turn and to >= T_VCM else 0
                    last = A(kept[:, b, to:to + width], ps[:, 4 * (k % 2) + b, c:c + width], ACT.Copy)
                last.then_inc(s_in_copied, 1)

            act.wait_ge(s_ones, 1)
            for layer in range(DEPTH):
                done[0] = 0
                split_to(layer, RING)
                scale_x(layer, 0)
                act.wait_ge(s_const_in, 32)
                act.wait_ge(s_params, nth("params", layer, PER_LAYER["params"]))
                A(gw_hi[:], gw_raw[:], ACT.Copy).then_inc(s_gw_hi, 1)
                for n in range(1, U_OUT):
                    if n == 4:
                        act.wait_ge(s_par_turned, nth("par_turned", layer, 1))
                        A(lnp[:].rearrange("p a k -> p (a k)"), ps[:, 4, 0:32], ACT.Copy)
                        A(pe_t[:].rearrange("p a l -> p (a l)"), ps[:, 4, 32:96], ACT.Copy).then_inc(s_par_ready, 1)
                    split_to(layer, n + RING)
                    if n >= 4:
                        act.wait_ge(s_unit_used, nth("unit_used", layer, n // 4 * 4))
                        copy_in(layer, n // 4 - 1, n % 4)
                split_to(layer, U_OUT + RING)
                act.wait_ge(s_unit_used, nth("unit_used", layer, U_OUT))
                for b in range(TT):
                    copy_in(layer, 4, b)
                for n in (1, 3):
                    q, bank = TURN_A[n]
                    act.wait_ge(s_turned, nth("turned", layer, n + 1))
                    for m in range(4):
                        last = A(ka_slot(2 * (q - Q_KA) + m // 2, m % 2), ps[:, bank, :], ACT.Identity,
                                 scale=kc[:, K_ROWS + m:K_ROWS + m + 1], bias=lams[:, 6:7])
                    last.then_inc(s_turned_act, 1)
                    if n == 1:
                        act.wait_ge(s_gates_done, nth("gates_done", layer, 1))
                        A(gates_t[0:GATES, :], ps[0:GATES, 7, :], ACT.Exp, scale=-1.0) \
                            .then_inc(s_exp_gates, 1)
                        act.wait_ge(s_lam_dot, nth("lam_dot", layer, 1))
                        A(lams[:, 2:4], lams[:, 0:2], ACT.Exp).then_inc(s_lam_exp, 1)

                def side(t):
                    n, (kind, c) = SIDE_NUMBER[t], SIDE[t]
                    if kind not in ("turn", "compress", "cmp_turn"):
                        return
                    act.wait_ge(s_side_ready, nth("side_ready", layer, n + 1))
                    b = ps[:, 7, :]
                    if kind == "compress":
                        A(kcmp[0:64, 0:32], b[0:64, 0:32], ACT.Copy)
                        A(kcmp[64:P, 32:64], b[0:64, 32:64], ACT.Copy)
                        A(vcmp[0:64, :], b[64:P, 64:P], ACT.Copy)
                        last = A(vcmp[64:P, :], b[64:P, 64:P], ACT.Copy)
                    elif kind == "cmp_turn":
                        src = b.rearrange("p (i m q) -> p i m q", i=2, m=2)
                        A(cmp_pt[:, 2 * c:2 * c + 2, 0, :], src[:, :, 0, :], ACT.Copy)
                        last = A(cmp_pt[0:64, 2 * c:2 * c + 2, 1, :], src[0:64, :, 1, :], ACT.Copy)
                    elif c >= Q_KSL:
                        for g in range(2):
                            last = A(qkt[:, (S_KSL if c == Q_KSL else S_KWI) + g, :], b, ACT.Identity,
                                     scale=kc[:, K_ROWS + 4 + g:K_ROWS + 5 + g], bias=lams[:, 6:7])
                    elif Q_U <= c < Q_QC:
                        last = A(upad[:, c - Q_U, 16:16 + SEQ], b, ACT.Copy)
                    else:
                        last = A(qkt[:, {Q_VCM: S_VCM, Q_KCM: S_KCM}.get(c, c - Q_QC + S_QC), :], b, ACT.Copy)
                    last.then_inc(s_side_emptied, 1)

                def exps(t):
                    n = P * (t % TT + 1)
                    act.wait_ge(s_negmax, nth("negmax", layer, t + 1))
                    if t >= 2:
                        act.wait_ge(s_p_turned, nth("p_turned", layer, t - 1))
                    for m in range(2):
                        last = A(probs[:, t % 2, m, 0:n], ps[:, 2 * (t % 2) + m, 0:n], ACT.Exp,
                                 bias=negmax[:, t % 4, m:m + 1], accum_out=sums[:, t % 4, m:m + 1])
                    last.then_inc(s_exped, 1)

                def copy_p(t):
                    n = P * (t % TT + 1)
                    act.wait_ge(s_p_turned, nth("p_turned", layer, t + 1))
                    if t >= 2:
                        act.wait_ge(s_pv, nth("pv", layer, t - 1))
                    if t < TASKS_A:
                        A(p_t[:, 0, t % 2, 0:n], ps[:, 4 + t % 2, 0:n], ACT.Copy).then_inc(s_p_copied, 1)
                    else:
                        A(p_t[:, :, t % 2, 0:n], ps[:, 4:6, 0:n], ACT.Copy).then_inc(s_p_copied, 1)

                def oc_high(pair):
                    act.wait_ge(s_pv, nth("pv", layer, TASKS_A + 8 * pair + 8))
                    A(mt_hi[:, 5 + pair], ps[:, 6 + pair % 2, :], ACT.Copy).then_inc(s_oc_hi, 1)

                for t in range(TASKS):
                    exps(t)
                    if t == 14:
                        act.wait_ge(s_cmp_shifted, nth("cmp_shifted", layer, 1))
                        flat = cmp_s[:].rearrange("p s n -> p (s n)")
                        A(flat, flat, ACT.Exp).then_inc(s_cmp_exp, 1)
                    if t:
                        copy_p(t - 1)
                    if t - 1 in SIDE:
                        side(t - 1)
                    if t in (9, 17, 25):
                        pair = t // 8 - 1
                        act.wait_ge(s_pv, nth("pv", layer, 8 * pair + 8))
                        A(oa[:, pair], ps[:, 6, :], ACT.Copy).then_inc(s_oa_copied, 1)
                        A(rms[:, pair], ps[:, 6, :], ACT.Square).then_inc(s_oa_squared, 1)
                    if t in (24, 25):
                        act.wait_ge(s_side_emptied, nth("side_emptied", layer, SIDE_NUMBER[t - 2] + 1))
                        A(mt_hi[:, 3 + t - 24], pooled[:, t - 24], ACT.Copy).then_inc(s_pool_hi, 1)
                    if t == 29:
                        act.wait_ge(s_side_emptied, nth("side_emptied", layer, len(SIDE)))
                        flat = rms[:].rearrange("p a q -> p (a q)")
                        A(flat, flat, ACT.Ln).then_inc(s_chain_act, 1)
                        act.wait_ge(s_chain_act, layer + 1)
                        A(flat, flat, ACT.Exp, scale=-0.5).then_inc(s_rms_ready, 1)
                    if 31 <= t <= 33:
                        act.wait_ge(s_oa_normed, nth("oa_normed", layer, t - 30))
                        A(mt_hi[:, t - 31], oa[:, t - 31], ACT.Copy).then_inc(s_oa_hi, 1)
                    if t in (33, 41):
                        oc_high(t // 8 - 4)
                copy_p(TASKS - 1)
                oc_high(2)
                act.wait_ge(s_oa_mixed, nth("oa_mixed", layer, 3))
                for n, a in enumerate((ln1_g, ln1_b)):
                    act.dma_start(rows[:, n], a[layer:layer + 1, :].to_broadcast([P, D])).then_inc(s_rows, 16)
                for n in range(U_OUT, U_MLP):
                    split_to(layer, n + RING)
                split_to(layer, U_MLP + RING)
                scale_x(layer, 1)
                for k in range(N_MLP):
                    if k == 2:
                        act.wait_ge(s_rows_used, nth("rows_used", layer, 1))
                        for n, a in enumerate((ln2_g, ln2_b)):
                            act.dma_start(rows[:, n], a[layer:layer + 1, :].to_broadcast([P, D])).then_inc(s_rows, 16)
                    kind, c = MLP[k - 1] if k else ("", 0)
                    for b in range(4):
                        split_to(layer, U_MLP + 4 * k + b + RING)
                        if kind == "up":
                            g, f = c // 2, 4 * (c % 2) + b
                            if g >= 2 and f == 0:
                                used = U_MLP + 4 * (MLP.index(("down", 2 * (g - 2) + 1)) + 1)
                                act.wait_ge(s_unit_used, nth("unit_used", layer, used))
                            act.wait_ge(s_mlp_evac, nth("mlp_evac", layer, 4 * (k - 1) + b + 1))
                            A((mt_hi if g % 2 else he_hi)[:, f], tmp[:, f % 2], ACT.Copy).then_inc(s_hid_hi, 1)

        @block.vector
        def _(dve):
            V = nc.vector
            chain = [0]

            def link(ins):
                ins.then_inc(s_chain_dve, 1)
                chain[0] += 1
                dve.wait_ge(s_chain_dve, chain[0])

            def split_x(layer, ln):
                for kt in range(KT):
                    s = KT * ln + kt
                    dve.wait_ge(s_xt_scaled, nth("xt_scaled", layer, s + 1))
                    link(V.tensor_copy(xt_hi[:, kt], tmp[:, kt % 2]))
                    V.tensor_tensor(xt_lo[:, kt], tmp[:, kt % 2], xt_hi[:, kt].bitcast(F32), ALU.subtract) \
                        .then_inc(s_xt_ready, 1)

            def affine_rows(layer, ln):
                dve.wait_ge(s_rows, nth("rows", layer, 32 * (ln + 1)))
                for tt in range(TT):
                    link(V.tensor_tensor(xres[:, tt], xres[:, tt], rows[:, 0], ALU.mult))
                    last = V.tensor_tensor(xres[:, tt], xres[:, tt], rows[:, 1], ALU.add)
                    if ln:
                        last.then_inc(s_out_normed, 1)
                    elif tt == TT - 1:
                        last.then_inc(s_rows_used, 1)

            def half_stats(tt, half):
                return V.bn_stats(bst[:, tt, half, :], xres[:, tt, 512 * half:512 * half + 512])

            def normalise(layer, ln, tt):
                dve.wait_ge(s_rstd, nth("rstd", layer, TT * ln + tt + 1))
                V.tensor_scalar(xres[:, tt], xres[:, tt], mv[:, tt, 0:1], rstd[:, tt:tt + 1], ALU.subtract, ALU.mult) \
                    .then_inc(s_x_normed, 1)

            def finish_rows(layer, ln, add):
                for tt in range(TT):
                    if tt < 3:
                        dve.wait_ge(s_bank_done, nth("bank_done", layer, 3 * ln + tt + 1))
                    else:
                        dve.wait_ge(s_unit_used, nth("unit_used", layer, UNITS if ln else U_OUT + 8))
                    add(tt)
                    link(half_stats(tt, 1))
                    link(V.bn_aggr(mv[:, tt, :], bst[:, tt].rearrange("p a s -> p (a s)")))
                    V.tensor_scalar(mv[:, tt, 1:2], mv[:, tt, 1:2], LN_EPS, None, ALU.add).then_inc(s_stats, 1)
                    if tt:
                        normalise(layer, ln, tt - 1)
                normalise(layer, ln, TT - 1)

            V.memset(lams[:, 6:7], 0.0)
            V.memset(kcmp[:], 0.0).then_inc(s_kcmp_zero, 1)
            V.memset(lnp[:, 2, :], 1.0)
            V.memset(lnp[:, 3, :], 0.0).then_inc(s_ones, 1)
            for layer in range(DEPTH):
                split_x(layer, 0)
                if layer == 0:
                    dve.wait_ge(s_const_in, 32)
                    dve.wait_ge(s_ident_in, 16)
                    V.tensor_copy(ident16[:], ident)
                    V.tensor_copy(mask16[:], rows[:, 0, 0:P]).then_inc(s_masks, 1)
                if layer:
                    dve.wait_ge(s_xt_turned, nth("xt_turned", layer, KT))
                    affine_rows(layer - 1, 1)
                dve.wait_ge(s_gw_hi, nth("gw_hi", layer, 1))
                V.tensor_tensor(gw_lo[:], gw_raw[:], gw_hi[:].bitcast(F32), ALU.subtract).then_inc(s_gw_lo, 1)
                prod = bst[:].rearrange("p a b c -> p (a b c)")[:, 0:32]
                link(V.tensor_tensor(prod, lamv[:, 0], lamv[:, 1], ALU.mult))
                link(V.tensor_reduce(lams[:, 0:1], prod, AX.X, ALU.add))
                link(V.tensor_tensor(prod, lamv[:, 2], lamv[:, 3], ALU.mult))
                V.tensor_reduce(lams[:, 1:2], prod, AX.X, ALU.add) \
                    .then_inc(s_lam_dot, 1)
                V.tensor_scalar(subg[:, 1:2], subg[:, 0:1], kc[:, K_LAM + 2 * layer + 1:K_LAM + 2 * layer + 2], None, ALU.mult)
                dve.wait_ge(s_in_copied, nth("in_copied", layer, 2 * TT))
                for tt in range(TT):
                    rotate(V.tensor_tensor, link, tt, ((T_QA, 12, 32, R_CAQ, R_SAQ), (T_KA, 12, 32, R_CAK, R_SAK))).then_inc(s_roped_a, 1)
                    dve.wait_ge(s_roped_a, nth("roped_a", layer, tt + 1))
                dve.wait_ge(s_in_copied, nth("in_copied", layer, 4 * TT))
                for tt in range(TT):
                    rotate(V.tensor_tensor, link, tt, ((T_QC, 6, 64, R_CCQ, R_SCQ), (T_KCM, 2, 64, R_CCK, R_SCK))).then_inc(s_roped_c, 1)
                    dve.wait_ge(s_roped_c, nth("roped_c", layer, tt + 1))
                dve.wait_ge(s_gates_done, nth("gates_done", layer, 1))
                for n, (q, bank) in enumerate(TURN_A):
                    if n in (1, 3):
                        continue
                    dve.wait_ge(s_turned, nth("turned", layer, n + 1))
                    if q < Q_KA:
                        last = V.tensor_copy(qkt[:, S_QA + q, :], ps[:, bank, :])
                    else:
                        for m in range(4):
                            last = V.tensor_scalar(ka_slot(2 * (q - Q_KA) + m // 2, m % 2), ps[:, bank, :],
                                                   kc[:, K_ROWS + m:K_ROWS + m + 1], None, ALU.mult)
                    last.then_inc(s_turned_dve, 1)
                dve.wait_ge(s_lam_exp, nth("lam_exp", layer, 1))
                link(V.tensor_tensor(lams[:, 4:5], lams[:, 3:4], lams[:, 2:3], ALU.subtract))
                link(V.tensor_tensor(lams[:, 5:6], lams[:, 4:5], kc[:, K_LAM + 2 * layer:K_LAM + 2 * layer + 1], ALU.subtract))

                def negative_max(t):
                    n = P * (t % TT + 1)
                    dve.wait_ge(s_scores, nth("scores", layer, t + 1))
                    b = 2 * (t % 2)
                    V.tensor_reduce(negmax[:, t % 4, :], ps[:, b:b + 2, 0:n], AX.X, ALU.max, negate=True) \
                        .then_inc(s_negmax, 1)

                def over24(a):
                    return cst[:, a, :].unsqueeze(2).to_broadcast([P, TT * 6, 32])

                def side(t):
                    n, (kind, c) = SIDE_NUMBER[t], SIDE[t]
                    if kind not in ("cmp_scores", "square_sums", "pool", "gates"):
                        return
                    dve.wait_ge(s_side_ready, nth("side_ready", layer, n + 1))
                    if kind == "cmp_scores":
                        cb = kc[:, K_CB + 64 * c:K_CB + 64 * c + 64].rearrange("p (i n) -> p i n", i=2).unsqueeze(2) \
                            .to_broadcast([P, 2, 6, 32])
                        V.tensor_tensor(cmp_s[:, 12 * c:12 * c + 12, :].rearrange("p (i s) n -> p i s n", i=2),
                                        ps[:, 7, 0:384].rearrange("p (i s n) -> p i s n", i=2, n=32), cb, ALU.add) \
                            .then_inc(s_side_emptied, 1)
                    elif kind == "gates":
                        V.tensor_scalar(gates[:].rearrange("p a g -> p (a g)"), ps[:, 7, 0:TT * GATES], 1.0, None, ALU.add) \
                            .then_inc(s_side_emptied, 1)
                        dve.wait_ge(s_side_emptied, nth("side_emptied", layer, n + 1))
                        link(V.reciprocal(gates[:], gates[:]))
                    elif kind == "square_sums":
                        V.tensor_scalar(rms[:, c], ps[:, 7, :], 1.0 / DV, RMS_EPS, ALU.mult, ALU.add) \
                            .then_inc(s_side_emptied, 1)
                    else:
                        V.tensor_scalar(pooled[:, c], ps[:, 7, :], psc[:, c:c + 1], None, ALU.mult) \
                            .then_inc(s_side_emptied, 1)

                def weights(t):
                    h, i = (t // TT) % 6, t % TT
                    n, s = P * (i + 1), t % 4
                    dve.wait_ge(s_exped, nth("exped", layer, t + 1))
                    p0, p1 = probs[:, t % 2, 0, 0:n], probs[:, t % 2, 1, 0:n]
                    link(V.reciprocal(recs[:, s, :], sums[:, s, :]))
                    if t < TASKS_A:
                        V.tensor_tensor(facs[:, s, 0:1], recs[:, s, 1:2], lams[:, 5:6], ALU.mult)
                        link(V.tensor_scalar(p0, p0, recs[:, s, 0:1], None, ALU.mult))
                        last = V.scalar_tensor_tensor(p0, p1, facs[:, s, 0:1], p0, ALU.mult, ALU.add)
                    else:
                        link(V.tensor_tensor(facs[:, s, :], recs[:, s, :], gates[:, i, 3 * h + 1:3 * h + 3], ALU.mult))
                        V.tensor_scalar(p0, p0, facs[:, s, 0:1], None, ALU.mult)
                        last = V.tensor_scalar(p1, p1, facs[:, s, 1:2], None, ALU.mult)
                    last.then_inc(s_probs, 1)

                def oc_low(pair):
                    dve.wait_ge(s_oc_hi, nth("oc_hi", layer, pair + 1))
                    V.tensor_tensor(mt_lo[:, 5 + pair], ps[:, 6 + pair % 2, :], mt_hi[:, 5 + pair].bitcast(F32),
                                    ALU.subtract).then_inc(s_oc_mixed, 1)

                negative_max(0)
                for t in range(TASKS):
                    if t + 1 < TASKS:
                        negative_max(t + 1)
                    weights(t)
                    if t - 1 in SIDE:
                        side(t - 1)
                    if t == 13:
                        dve.wait_ge(s_side_emptied, nth("side_emptied", layer, SIDE_NUMBER[11] + 1))
                        link(V.tensor_reduce(cst[:, 0, :], cmp_s[:], AX.X, ALU.max))
                        V.tensor_tensor(cmp_s[:], cmp_s[:], over24(0), ALU.subtract).then_inc(s_cmp_shifted, 1)
                    if t == 15:
                        dve.wait_ge(s_cmp_exp, nth("cmp_exp", layer, 1))
                        link(V.tensor_reduce(cst[:, 1, :], cmp_s[:], AX.X, ALU.add))
                        link(V.reciprocal(cst[:, 2, :], cst[:, 1, :]))
                        gv = gates[:].rearrange("p i (g j r) -> p i j g r", g=2, r=3)[:, :, :, :, 0]
                        fv = cst[:, 2, :].rearrange("p (i j g) -> p i j g", i=TT, j=HG)
                        ov = cst[:, 3, :].rearrange("p (i j g) -> p i j g", i=TT, j=HG)
                        V.tensor_tensor(ov, fv, gv, ALU.mult)
                        cm = kc[:, K_CM:K_CM + TT * 32].rearrange("p (i n) -> p i n", i=TT).unsqueeze(2) \
                            .to_broadcast([P, TT, 6, 32])
                        cv = cmp_s[:].rearrange("p (i s) n -> p i s n", i=TT)
                        link(V.tensor_tensor(cv, cv, cm, ALU.mult))
                        V.tensor_tensor(cmp_s[:], cmp_s[:], over24(3), ALU.mult).then_inc(s_cmp_probs, 1)
                    if t in (25, 26):
                        c = t - 25
                        dve.wait_ge(s_pool_hi, nth("pool_hi", layer, c + 1))
                        V.tensor_tensor(mt_lo[:, 3 + c], pooled[:, c], mt_hi[:, 3 + c].bitcast(F32),
                                        ALU.subtract).then_inc(s_pool_mixed, 1)
                    if t == 30:
                        dve.wait_ge(s_rms_ready, nth("rms_ready", layer, 1))
                    if 30 <= t <= 32:
                        V.scalar_tensor_tensor(oa[:, t - 30], oa[:, t - 30], subg[:, 1:2], rms[:, t - 30], ALU.mult, ALU.mult) \
                            .then_inc(s_oa_normed, 1)
                    if 32 <= t <= 34:
                        dve.wait_ge(s_oa_hi, nth("oa_hi", layer, t - 31))
                        V.tensor_tensor(mt_lo[:, t - 32], oa[:, t - 32], mt_hi[:, t - 32].bitcast(F32), ALU.subtract) \
                            .then_inc(s_oa_mixed, 1)
                    if t in (34, 42):
                        oc_low(t // 8 - 4)
                oc_low(2)
                def add_bank(tt, half, bank, alpha):
                    xs = xres[:, tt, 512 * half:512 * half + 512]
                    if alpha:
                        return V.scalar_tensor_tensor(xs, xs, ALPHA, ps[:, bank + tt, :], ALU.mult, ALU.add)
                    return V.tensor_tensor(xs, xs, ps[:, bank + tt, :], ALU.add)

                dve.wait_ge(s_unit_used, nth("unit_used", layer, U_OUT + 4))
                for tt in range(TT):
                    link(add_bank(tt, 0, 0, True))
                    half_stats(tt, 0)
                finish_rows(layer, 0, lambda tt: link(add_bank(tt, 1, 4, True)))
                split_x(layer, 1)
                dve.wait_ge(s_xt_turned, nth("xt_turned", layer, 2 * KT))
                affine_rows(layer, 0)
                for k, (kind, c) in enumerate(MLP):
                    bank = 4 * ((k + 1) % 2)
                    if k < N_MLP - 1:
                        dve.wait_ge(s_unit_used, nth("unit_used", layer, U_MLP + 4 * (k + 1)))
                    if kind == "up":
                        g = c // 2
                        hi, lo = (mt_hi, mt_lo) if g % 2 else (he_hi, he_lo)

                        def low(b):
                            f = 4 * (c % 2) + b
                            dve.wait_ge(s_hid_hi, nth("hid_hi", layer, 4 * c + b + 1))
                            V.tensor_tensor(lo[:, f], tmp[:, f % 2], hi[:, f].bitcast(F32), ALU.subtract) \
                                .then_inc(s_hid_ready, 1)

                        for b in range(4):
                            f = 4 * (c % 2) + b
                            if 4 * c + b >= 2:
                                dve.wait_ge(s_hid_ready, nth("hid_ready", layer, 4 * c + b - 1))
                            link(V.tensor_scalar(tmp[:, f % 2], ps[:, bank + b, :], 0.0, None, ALU.max))
                            V.tensor_tensor(tmp[:, f % 2], tmp[:, f % 2], ps[:, bank + b, :], ALU.mult) \
                                .then_inc(s_mlp_evac, 1)
                            if b:
                                low(b - 1)
                        low(3)
                    else:
                        g, half = c // 2, c % 2

                        def add(tt):
                            add_bank(tt, half, bank, g == 0).then_inc(s_mlp_evac, 1)
                            dve.wait_ge(s_mlp_evac, nth("mlp_evac", layer, 4 * k + tt + 1))

                        if k < N_MLP - 1:
                            for tt in range(TT):
                                add(tt)
                                if k == N_MLP - 2:
                                    half_stats(tt, 0)
                        else:
                            finish_rows(layer, 1, add)
            affine_rows(DEPTH - 1, 1)


INPUTS = ("x", "w_in", "lam_q1", "lam_k1", "lam_q2", "lam_k2", "subln_g", "w_pool", "pool_scale", "cmp_pe_k",
          "cmp_pe_v", "w_cmp_k", "w_cmp_v", "w_out", "ln1_g", "ln1_b", "w_up", "w_down", "ln2_g", "ln2_b")


def kernel(**inputs):
    import concourse.bacc as bacc
    from concourse.bass_utils import run_bass_kernel_spmd

    nc = bacc.Bacc("TRN2", target_bir_lowering=False, num_devices=1)
    arrays, args = {}, []
    for name in INPUTS + ("consts",):
        a = np.ascontiguousarray(shape_constants() if name == "consts" else inputs[name])
        arrays[f"in_{name}"] = a
        args.append(nc.dram_tensor(f"in_{name}", a.shape, mybir.dt.from_np(a.dtype), kind="ExternalInput").ap())
    args.append(nc.dram_tensor("out_x", (1, SEQ, D), F32, kind="ExternalOutput").ap())
    build(nc, *args)
    r = run_bass_kernel_spmd(nc, [arrays], core_ids=[0])
    return r.results[0]["out_x"]
```
